# Optimizing a Trainium2 kernel written in Bass

```python
import math
import jax, jax.numpy as jnp
from jax import lax
import numpy as np

D_MODEL = 1024
BATCH = 1
SEQ = 256
DEPTH = 2

GRID_W = 64
CTX_LEN = 256
N_MIXERS = 2
N_HEADS = 16
HEAD_DIM = D_MODEL // N_HEADS
NA_KH = 8
NA_KW = 16
SWA_KV_HEADS = 4
SWA_GROUP = N_HEADS // SWA_KV_HEADS
SWA_WINDOW = 128
SWA_BLOCK = 128
D_FF = 4 * D_MODEL
ROPE_BASE = 10000.0
NORM_EPS = 1e-6
NEG_INF = -1e30
N_NA_LAYERS = (DEPTH + 1) // 2
N_SWA_LAYERS = DEPTH // 2


def rms_norm(x, g):
    xf = x.astype(jnp.float32)
    y = xf * lax.rsqrt(jnp.mean(xf * xf, axis=-1, keepdims=True) + NORM_EPS)
    return (y * g.astype(jnp.float32)).astype(x.dtype)

def modulate(h, shift, scale):
    return h * (1 + scale) + shift

def squared_relu_mlp(h, w1, w2):
    return jnp.square(jax.nn.relu(h @ w1)) @ w2

def axial_rope_tables(L):
    t = jnp.arange(L, dtype=jnp.int32)
    row = (t // GRID_W).astype(jnp.float32)
    col = (t % GRID_W).astype(jnp.float32)
    n_freq = HEAD_DIM // 4
    inv = ROPE_BASE ** (-jnp.arange(n_freq, dtype=jnp.float32) / n_freq)
    ang = jnp.stack([row[:, None] * inv, col[:, None] * inv], axis=1)
    return jnp.cos(ang), jnp.sin(ang)

def apply_axial_rope(x, cos, sin):
    B, L, h, dh = x.shape
    xr = x.astype(jnp.float32).reshape(B, L, h, 2, 2, dh // 4)
    x1, x2 = xr[..., 0, :], xr[..., 1, :]
    cb = cos[None, :, None]
    sb = sin[None, :, None]
    out = jnp.stack([x1 * cb - x2 * sb, x1 * sb + x2 * cb], axis=-2)
    return out.reshape(B, L, h, dh).astype(x.dtype)

def context_attention(q, k, v, sink=None):
    B, C, KV, G, dh = q.shape
    s = jnp.einsum('bqkgd,bskd->bkgqs', q, k, preferred_element_type=jnp.float32) * (dh ** -0.5)
    if sink is not None:
        s_sink = jnp.broadcast_to(sink.reshape(1, KV, G, 1, 1).astype(jnp.float32), (B, KV, G, C, 1))
        s = jnp.concatenate([s, s_sink], axis=-1)
    p = jax.nn.softmax(s, axis=-1)[..., :C].astype(v.dtype)
    o = jnp.einsum('bkgqs,bskd->bqkgd', p, v)
    return o.reshape(B, C, KV * G * dh)

def neighborhood_attention(q, k, v, kc, vc, rpb):
    B, L, H, dh = q.shape
    rows = L // GRID_W
    kh = min(NA_KH, rows)
    kw = min(NA_KW, GRID_W)
    n_loc = kh * kw
    scale = dh ** -0.5
    qg = q.reshape(B, rows, GRID_W, H, dh)
    kg = k.reshape(B, rows, GRID_W, H, dh)
    vg = v.reshape(B, rows, GRID_W, H, dh)
    cols = jnp.arange(GRID_W)
    col_start = jnp.clip(cols - kw // 2, 0, GRID_W - kw)
    col_idx = col_start[:, None] + jnp.arange(kw)[None, :]
    col_off = col_idx - cols[:, None] + (NA_KW - 1)

    def one_row(r):
        r0 = jnp.clip(r - kh // 2, 0, rows - kh)
        k_rows = lax.dynamic_slice_in_dim(kg, r0, kh, axis=1)
        v_rows = lax.dynamic_slice_in_dim(vg, r0, kh, axis=1)
        k_win = k_rows[:, :, col_idx]
        v_win = v_rows[:, :, col_idx]
        q_row = lax.dynamic_index_in_dim(qg, r, axis=1, keepdims=False)
        s_loc = jnp.einsum('bqhd,bkqwhd->bhqkw', q_row, k_win,
                           preferred_element_type=jnp.float32) * scale
        row_off = r0 + jnp.arange(kh) - r + (NA_KH - 1)
        bias = rpb[:, row_off[:, None, None], col_off[None, :, :]]
        s_loc = s_loc + jnp.transpose(bias, (0, 2, 1, 3)).astype(jnp.float32)[None]
        s_ctx = jnp.einsum('bqhd,bchd->bhqc', q_row, kc,
                           preferred_element_type=jnp.float32) * scale
        s = jnp.concatenate([s_loc.reshape(B, H, GRID_W, n_loc), s_ctx], axis=-1)
        p = jax.nn.softmax(s, axis=-1).astype(v.dtype)
        p_loc = p[..., :n_loc].reshape(B, H, GRID_W, kh, kw)
        p_ctx = p[..., n_loc:]
        return (jnp.einsum('bhqkw,bkqwhd->bqhd', p_loc, v_win)
                + jnp.einsum('bhqc,bchd->bqhd', p_ctx, vc))

    out = lax.map(one_row, jnp.arange(rows))
    return jnp.transpose(out, (1, 0, 2, 3, 4)).reshape(B, L, H * dh)

def sliding_window_attention(q, k, v, kc, vc, sink):
    B, L, KV, G, dh = q.shape
    C = kc.shape[1]
    T = SWA_BLOCK
    nb = L // T
    scale = dh ** -0.5
    qb = q.reshape(B, nb, T, KV, G, dh)
    pad = jnp.zeros((B, T, KV, dh), k.dtype)
    kp = jnp.concatenate([pad, k, pad], axis=1)
    vp = jnp.concatenate([pad, v, pad], axis=1)
    rel = (jnp.arange(3 * T)[None, :] - T) - jnp.arange(T)[:, None]
    s_sink = jnp.broadcast_to(sink.reshape(1, KV, G, 1, 1).astype(jnp.float32), (B, KV, G, T, 1))

    def one_block(j):
        q_blk = lax.dynamic_index_in_dim(qb, j, axis=1, keepdims=False)
        k_blk = lax.dynamic_slice_in_dim(kp, j * T, 3 * T, axis=1)
        v_blk = lax.dynamic_slice_in_dim(vp, j * T, 3 * T, axis=1)
        kpos = (j - 1) * T + jnp.arange(3 * T)
        valid = (jnp.abs(rel) <= SWA_WINDOW) & ((kpos >= 0) & (kpos < L))[None, :]
        s_loc = jnp.einsum('bqkgd,bskd->bkgqs', q_blk, k_blk,
                           preferred_element_type=jnp.float32) * scale
        s_loc = jnp.where(valid, s_loc, NEG_INF)
        s_ctx = jnp.einsum('bqkgd,bckd->bkgqc', q_blk, kc,
                           preferred_element_type=jnp.float32) * scale
        s = jnp.concatenate([s_loc, s_ctx, s_sink], axis=-1)
        p = jax.nn.softmax(s, axis=-1).astype(v.dtype)
        return (jnp.einsum('bkgqs,bskd->bqkgd', p[..., :3 * T], v_blk)
                + jnp.einsum('bkgqc,bckd->bqkgd', p[..., 3 * T:3 * T + C], vc))

    out = lax.map(one_block, jnp.arange(nb))
    return jnp.transpose(out, (1, 0, 2, 3, 4, 5)).reshape(B, L, KV * G * dh)

def first_inputs(seed: int = 0) -> dict:
    key = jax.random.key(seed)
    ks = jax.random.split(key, 24)
    f = jnp.float32
    d = D_MODEL
    kv_w = SWA_KV_HEADS * HEAD_DIM

    def nrm(k, shape, scale):
        return jax.random.normal(k, shape, f) * scale

    return {
        "x": nrm(ks[0], (BATCH, SEQ, d), 1.0),
        "c": nrm(ks[1], (BATCH, d), 1.0),
        "ctx": nrm(ks[2], (BATCH, CTX_LEN, d), 1.0),
        "c_ctx": nrm(ks[3], (d,), 1.0),
        "ada_w": nrm(ks[4], (DEPTH, d, 6 * d), 0.5 * d ** -0.5),
        "ada_b": nrm(ks[5], (DEPTH, 6 * d), 0.02),
        "g_mix": 1.0 + nrm(ks[6], (DEPTH, d), 0.02),
        "g_mlp": 1.0 + nrm(ks[7], (DEPTH, d), 0.02),
        "mlp_w1": nrm(ks[8], (DEPTH, d, D_FF), d ** -0.5),
        "mlp_w2": nrm(ks[9], (DEPTH, D_FF, d), D_FF ** -0.5),
        "na_wqkv": nrm(ks[10], (N_NA_LAYERS, d, 3 * d), d ** -0.5),
        "na_q_gain": 1.0 + nrm(ks[11], (N_NA_LAYERS, HEAD_DIM), 0.02),
        "na_k_gain": 1.0 + nrm(ks[12], (N_NA_LAYERS, HEAD_DIM), 0.02),
        "na_rpb": nrm(ks[13], (N_NA_LAYERS, N_HEADS, 2 * NA_KH - 1, 2 * NA_KW - 1), 0.1),
        "na_wo": nrm(ks[14], (N_NA_LAYERS, d, d), d ** -0.5),
        "swa_wqkv": nrm(ks[15], (N_SWA_LAYERS, d, d + 2 * kv_w), d ** -0.5),
        "swa_q_gain": 1.0 + nrm(ks[16], (N_SWA_LAYERS, HEAD_DIM), 0.02),
        "swa_k_gain": 1.0 + nrm(ks[17], (N_SWA_LAYERS, HEAD_DIM), 0.02),
        "swa_sink": nrm(ks[18], (N_SWA_LAYERS, N_HEADS), 0.5),
        "swa_wo": nrm(ks[19], (N_SWA_LAYERS, d, d), d ** -0.5),
    }

def first_block(x, c, ctx, c_ctx, ada_w, ada_b, g_mix, g_mlp, mlp_w1, mlp_w2,
              na_wqkv, na_q_gain, na_k_gain, na_rpb, na_wo,
              swa_wqkv, swa_q_gain, swa_k_gain, swa_sink, swa_wo):
    B, L, D = x.shape
    C = ctx.shape[1]
    H, dh, KV, G = N_HEADS, HEAD_DIM, SWA_KV_HEADS, SWA_GROUP
    cos, sin = axial_rope_tables(L)
    silu_c = jax.nn.silu(c)
    silu_cc = jax.nn.silu(c_ctx)
    h_lat = x
    h_ctx = ctx
    for i in range(DEPTH):
        last = i == DEPTH - 1
        j = i // N_MIXERS
        mod_lat = (silu_c @ ada_w[i] + ada_b[i])[:, None, :]
        mod_ctx = (silu_cc @ ada_w[i] + ada_b[i])[None, None, :]
        sh1, sc1, ga1, sh2, sc2, ga2 = jnp.split(mod_lat, 6, axis=-1)
        csh1, csc1, cga1, csh2, csc2, cga2 = jnp.split(mod_ctx, 6, axis=-1)
        u_lat = modulate(rms_norm(h_lat, g_mix[i]), sh1, sc1)
        u_ctx = modulate(rms_norm(h_ctx, g_mix[i]), csh1, csc1)

        if i % N_MIXERS == 0:
            w = na_wqkv[j]
            ql, kl, vl = jnp.split((u_lat @ w).reshape(B, L, 3, H, dh), 3, axis=2)
            qc, kc, vc = jnp.split((u_ctx @ w).reshape(B, C, 3, H, dh), 3, axis=2)
            ql, kl, vl = ql[:, :, 0], kl[:, :, 0], vl[:, :, 0]
            qc, kc, vc = qc[:, :, 0], kc[:, :, 0], vc[:, :, 0]
            ql, qc = rms_norm(ql, na_q_gain[j]), rms_norm(qc, na_q_gain[j])
            kl, kc = rms_norm(kl, na_k_gain[j]), rms_norm(kc, na_k_gain[j])
            y_lat = neighborhood_attention(ql, kl, vl, kc, vc, na_rpb[j]) @ na_wo[j]
            if not last:
                y_ctx = context_attention(qc[:, :, :, None, :], kc, vc) @ na_wo[j]
        else:
            w = swa_wqkv[j]
            pl = u_lat @ w
            pc = u_ctx @ w
            kvw = KV * dh
            ql = pl[..., :D].reshape(B, L, H, dh)
            kl = pl[..., D:D + kvw].reshape(B, L, KV, dh)
            vl = pl[..., D + kvw:].reshape(B, L, KV, dh)
            qc = pc[..., :D].reshape(B, C, H, dh)
            kc = pc[..., D:D + kvw].reshape(B, C, KV, dh)
            vc = pc[..., D + kvw:].reshape(B, C, KV, dh)
            ql, qc = rms_norm(ql, swa_q_gain[j]), rms_norm(qc, swa_q_gain[j])
            kl, kc = rms_norm(kl, swa_k_gain[j]), rms_norm(kc, swa_k_gain[j])
            ql = apply_axial_rope(ql, cos, sin)
            kl = apply_axial_rope(kl, cos, sin)
            y_lat = sliding_window_attention(ql.reshape(B, L, KV, G, dh), kl, vl,
                                             kc, vc, swa_sink[j]) @ swa_wo[j]
            if not last:
                y_ctx = context_attention(qc.reshape(B, C, KV, G, dh), kc, vc,
                                          sink=swa_sink[j]) @ swa_wo[j]

        h_lat = h_lat + ga1 * y_lat
        h_lat = h_lat + ga2 * squared_relu_mlp(
            modulate(rms_norm(h_lat, g_mlp[i]), sh2, sc2), mlp_w1[i], mlp_w2[i])
        if not last:
            h_ctx = h_ctx + cga1 * y_ctx
            h_ctx = h_ctx + cga2 * squared_relu_mlp(
                modulate(rms_norm(h_ctx, g_mlp[i]), csh2, csc2), mlp_w1[i], mlp_w2[i])
    return h_lat


CHUNK = 64
Q_BLOCK = 128
N_A_LAYERS = DEPTH // 2
N_B_LAYERS = DEPTH - N_A_LAYERS
SSM_GROUP = 16
N_GROUPS = D_MODEL // SSM_GROUP
SSM_STATE = 64
HEAD_DIM_2 = 64
N_HEADS_2 = D_MODEL // HEAD_DIM_2
D_FF_2 = 2816
CONV_W = 3
EPS = 1e-6
DT_MIN = 1e-3
DT_MAX = 1e-1


def rms_norm_2(x, g):
    xf = x.astype(jnp.float32)
    y = xf * lax.rsqrt(jnp.mean(xf * xf, axis=-1, keepdims=True) + EPS)
    return (y * g.astype(jnp.float32)).astype(x.dtype)

def s5_mixer(xn, w_in, lam_re, lam_im, b_re, b_im, c_re, c_im, d_skip, log_dt, w_glu):
    f32 = jnp.float32
    bsz, seq, _ = xn.shape
    u = (xn @ w_in).astype(f32)
    lam = lax.complex(lam_re.astype(f32), lam_im.astype(f32))
    dt = jnp.exp(log_dt.astype(f32))[:, None]
    a_bar = jnp.exp(lam * dt)
    b_mat = lax.complex(b_re.astype(f32), b_im.astype(f32))
    b_bar = ((a_bar - 1.0) / lam)[..., None] * b_mat
    c_mat = lax.complex(c_re.astype(f32), c_im.astype(f32))
    n_chunks = seq // CHUNK
    u_c = u.reshape(bsz, n_chunks, CHUNK, N_GROUPS, SSM_GROUP).transpose(1, 2, 0, 3, 4)
    a_elems = jnp.broadcast_to(a_bar, (CHUNK, 1, N_GROUPS, SSM_STATE))

    def binop(left, right):
        a_l, b_l = left
        a_r, b_r = right
        return a_r * a_l, a_r * b_l + b_r

    def chunk_step(h0, u_t):
        bu = jnp.einsum('tbgh,gph->tbgp', u_t.astype(jnp.complex64), b_bar)
        a_cum, s = lax.associative_scan(binop, (a_elems, bu), axis=0)
        s = s + a_cum * h0[None]
        y = jnp.einsum('tbgp,ghp->tbgh', s, c_mat).real
        return s[-1], y

    h0 = jnp.zeros((bsz, N_GROUPS, SSM_STATE), jnp.complex64)
    _, y = lax.scan(chunk_step, h0, u_c)
    y = y.transpose(2, 0, 1, 3, 4).reshape(bsz, seq, D_MODEL)
    y = y + d_skip.astype(f32) * u
    g = jax.nn.gelu(y).astype(xn.dtype)
    val, gate = jnp.split(g @ w_glu, 2, axis=-1)
    return val * jax.nn.sigmoid(gate)

def shared_kv(h, kv_norm, w_kv, k_norm):
    bsz, seq, _ = h.shape
    k, v = jnp.split(rms_norm_2(h, kv_norm) @ w_kv, 2, axis=-1)
    k = rms_norm_2(k.reshape(bsz, seq, N_HEADS_2, HEAD_DIM_2), k_norm)
    v = v.reshape(bsz, seq, N_HEADS_2, HEAD_DIM_2)
    return k, v

def stick_breaking_attention(q, k, v):
    seq = q.shape[1]
    scale = HEAD_DIM_2 ** -0.5
    outs = []
    for i in range(seq // Q_BLOCK):
        q0 = i * Q_BLOCK
        kv_len = q0 + Q_BLOCK
        z = jnp.einsum('bqhd,bkhd->bhqk', q[:, q0:kv_len], k[:, :kv_len]).astype(jnp.float32) * scale
        q_pos = q0 + jnp.arange(Q_BLOCK)[:, None]
        k_pos = jnp.arange(kv_len)[None, :]
        causal = k_pos < q_pos
        log_beta = jax.nn.log_sigmoid(z)
        log_1m = jnp.where(causal, log_beta - z, 0.0)
        later = lax.cumsum(log_1m, axis=3, reverse=True) - log_1m
        w = jnp.where(causal, jnp.exp(log_beta + later), 0.0)
        outs.append(jnp.einsum('bhqk,bkhd->bqhd', w.astype(v.dtype), v[:, :kv_len]))
    return jnp.concatenate(outs, axis=1)

def sb_mixer(xn, w_q, q_norm, k, v, w_o):
    bsz, seq, _ = xn.shape
    q = rms_norm_2((xn @ w_q).reshape(bsz, seq, N_HEADS_2, HEAD_DIM_2), q_norm)
    o = stick_breaking_attention(q, k, v)
    return o.reshape(bsz, seq, D_MODEL) @ w_o

def conv_ffn(xn, w_up, conv_w, conv_b, w_down):
    seq = xn.shape[1]
    val, gate = jnp.split(xn @ w_up, 2, axis=-1)
    gp = jnp.pad(gate, ((0, 0), (CONV_W - 1, 0), (0, 0)))
    gc = conv_b + conv_w[0] * gp[:, 0:seq]
    for j in range(1, CONV_W):
        gc = gc + conv_w[j] * gp[:, j:j + seq]
    return (jax.nn.silu(gc) * val) @ w_down

def second_inputs(seed: int = 0) -> dict:
    key = jax.random.key(seed)
    ks = iter(jax.random.split(key, 32))

    def nrm(shape, scale):
        return scale * jax.random.normal(next(ks), shape, jnp.float32)

    def gain(shape):
        return 1.0 + nrm(shape, 0.02)

    d, f = D_MODEL, D_FF_2
    na, nb = N_A_LAYERS, N_B_LAYERS
    G, P, H = N_GROUPS, SSM_STATE, SSM_GROUP
    n_idx = jnp.arange(P, dtype=jnp.float32)
    x = nrm((BATCH, SEQ, d), 1.0)
    a_norm = gain((na, d))
    a_w_in = nrm((na, d, d), d ** -0.5)
    a_lam_re = -0.5 + nrm((na, G, P), 0.01)
    a_lam_im = math.pi * n_idx + nrm((na, G, P), 0.01)
    a_b_re = nrm((na, G, P, H), (2 * H) ** -0.5)
    a_b_im = nrm((na, G, P, H), (2 * H) ** -0.5)
    a_c_re = nrm((na, G, H, P), P ** -0.5)
    a_c_im = nrm((na, G, H, P), P ** -0.5)
    a_d = nrm((na, d), 1.0)
    a_log_dt = jax.random.uniform(next(ks), (na, G), jnp.float32, math.log(DT_MIN), math.log(DT_MAX))
    a_w_glu = nrm((na, d, 2 * d), d ** -0.5)
    kv_norm = gain((d,))
    w_kv = nrm((d, 2 * d), d ** -0.5)
    k_norm = gain((HEAD_DIM_2,))
    b_norm = gain((nb, d))
    b_w_q = nrm((nb, d, d), d ** -0.5)
    b_q_norm = gain((nb, HEAD_DIM_2))
    b_w_o = nrm((nb, d, d), d ** -0.5)
    ffn_norm = gain((DEPTH, d))
    ffn_w_up = nrm((DEPTH, d, 2 * f), d ** -0.5)
    ffn_conv_w = nrm((DEPTH, CONV_W, f), CONV_W ** -0.5)
    ffn_conv_b = nrm((DEPTH, f), 0.02)
    ffn_w_down = nrm((DEPTH, f, d), f ** -0.5)
    return {"x": x, "a_norm": a_norm, "a_w_in": a_w_in, "a_lam_re": a_lam_re, "a_lam_im": a_lam_im,
            "a_b_re": a_b_re, "a_b_im": a_b_im, "a_c_re": a_c_re, "a_c_im": a_c_im, "a_d": a_d,
            "a_log_dt": a_log_dt, "a_w_glu": a_w_glu, "kv_norm": kv_norm, "w_kv": w_kv, "k_norm": k_norm,
            "b_norm": b_norm, "b_w_q": b_w_q, "b_q_norm": b_q_norm, "b_w_o": b_w_o,
            "ffn_norm": ffn_norm, "ffn_w_up": ffn_w_up, "ffn_conv_w": ffn_conv_w,
            "ffn_conv_b": ffn_conv_b, "ffn_w_down": ffn_w_down}

def second_block(x, a_norm, a_w_in, a_lam_re, a_lam_im, a_b_re, a_b_im, a_c_re, a_c_im, a_d,
              a_log_dt, a_w_glu, kv_norm, w_kv, k_norm, b_norm, b_w_q, b_q_norm, b_w_o,
              ffn_norm, ffn_w_up, ffn_conv_w, ffn_conv_b, ffn_w_down):
    h = x
    k = None
    v = None
    for layer in range(DEPTH):
        if layer < N_A_LAYERS:
            i = layer
            h = h + s5_mixer(rms_norm_2(h, a_norm[i]), a_w_in[i], a_lam_re[i], a_lam_im[i],
                             a_b_re[i], a_b_im[i], a_c_re[i], a_c_im[i], a_d[i], a_log_dt[i], a_w_glu[i])
        else:
            j = layer - N_A_LAYERS
            if j == 0:
                k, v = shared_kv(h, kv_norm, w_kv, k_norm)
            h = h + sb_mixer(rms_norm_2(h, b_norm[j]), b_w_q[j], b_q_norm[j], k, v, b_w_o[j])
        h = h + conv_ffn(rms_norm_2(h, ffn_norm[layer]), ffn_w_up[layer], ffn_conv_w[layer],
                         ffn_conv_b[layer], ffn_w_down[layer])
    return h


def setup_inputs(seed=0):
    out = dict(first_inputs(seed))
    for name, value in second_inputs(seed + 1).items():
        if name != "x":
            out[name + "_2"] = value
    return out


def reference(
    x, c, ctx, c_ctx, ada_w, ada_b, g_mix, g_mlp, mlp_w1, mlp_w2, na_wqkv, na_q_gain, na_k_gain,
    na_rpb, na_wo, swa_wqkv, swa_q_gain, swa_k_gain, swa_sink, swa_wo, a_norm_2, a_w_in_2,
    a_lam_re_2, a_lam_im_2, a_b_re_2, a_b_im_2, a_c_re_2, a_c_im_2, a_d_2, a_log_dt_2,
    a_w_glu_2, kv_norm_2, w_kv_2, k_norm_2, b_norm_2, b_w_q_2, b_q_norm_2, b_w_o_2, ffn_norm_2,
    ffn_w_up_2, ffn_conv_w_2, ffn_conv_b_2, ffn_w_down_2,
):
    x = first_block(
        x, c, ctx, c_ctx, ada_w, ada_b, g_mix, g_mlp, mlp_w1, mlp_w2, na_wqkv, na_q_gain,
        na_k_gain, na_rpb, na_wo, swa_wqkv, swa_q_gain, swa_k_gain, swa_sink, swa_wo,
    )
    return second_block(
        x, a_norm_2, a_w_in_2, a_lam_re_2, a_lam_im_2, a_b_re_2, a_b_im_2, a_c_re_2, a_c_im_2,
        a_d_2, a_log_dt_2, a_w_glu_2, kv_norm_2, w_kv_2, k_norm_2, b_norm_2, b_w_q_2,
        b_q_norm_2, b_w_o_2, ffn_norm_2, ffn_w_up_2, ffn_conv_w_2, ffn_conv_b_2, ffn_w_down_2,
    )


_drawn_inputs = setup_inputs


def setup_inputs(seed=0):
    import zlib

    import numpy as np

    out = dict(_drawn_inputs(seed))
    spreads = {}
    factors = {'g_mix': 8.0,
     'g_mlp': 3.649,
     'na_q_gain': 8.0,
     'na_k_gain': 8.0,
     'na_rpb': 8.0,
     'swa_q_gain': 8.0,
     'swa_k_gain': 8.0,
     'swa_sink': 8.0,
     'a_norm_2': 7.7,
     'a_lam_re_2': 8.0,
     'a_b_re_2': 2.789,
     'a_b_im_2': 2.826,
     'a_c_re_2': 2.765,
     'a_c_im_2': 2.716,
     'kv_norm_2': 5.629,
     'k_norm_2': 8.0,
     'b_norm_2': 8.0,
     'b_q_norm_2': 8.0,
     'ffn_norm_2': 3.197,
     'ffn_conv_b_2': 4.74}
    for name, (base, spread) in spreads.items():
        noise = np.random.default_rng([zlib.crc32(name.encode()), seed]).standard_normal(out[name].shape)
        drawn = base * np.exp(spread * noise) if base else spread * noise
        out[name] = __import__('jax').numpy.asarray(drawn.astype(out[name].dtype))
    for name, factor in factors.items():
        out[name] = (out[name] * factor).astype(out[name].dtype)
    return out
```

```python
from contextlib import ExitStack, contextmanager

import numpy as np

import concourse.bass as bass
from concourse import mybir

ALU = mybir.AluOpType
ACT = mybir.ActivationFunctionType
AX = mybir.AxisListType
F32 = mybir.dt.float32
F32R = mybir.dt.float32r

P = 128
D = 1024
KT = D // P
SEQ = 256
TOK = 2 * SEQ
HEADS = 16
HD = 64
DFF = 4096
HALF = DFF // 2 // P
DFF2 = 2816
FT = DFF2 // P
GRID_W = 64
UNIT = 1024
VW = 256
RING = 4
CREDIT = RING
EPS = 1e-6
NEG = -1e30
LOW = -43.0
INV_HD = 1.0 / HD
INV_D = 1.0 / D
GROUPS = 64
SSM_H = 16
STATES = 64
CH = 8
NCH = SEQ // CH
PAIRS = GROUPS // 2
QJ = 8
NQ = PAIRS // QJ
POW = CH + 1
N_ADA = 48


class Stage:

    def __init__(self, name, kind, tiles, units=1, tok=SEQ, ada=None, **more):
        self.name, self.kind, self.tiles, self.units, self.tok, self.ada = name, kind, tiles, units, tok, ada
        self.more = more
        self.base = {}


def increments(s):
    n = s.tiles
    c = {"unit": n * s.units}
    if s.kind == "QK":
        c.update(a1=n, d1=n, p2=n, a2=n, d2=n)
    elif s.kind == "IN":
        c.update(a1=n)
    elif s.kind == "V":
        c.update(a1=n // 2)
    elif s.kind == "RES":
        c.update(d1=n)
        if s.more.get("norm"):
            c.update(a1=n, sq=n, d3=n // 4)
    elif s.kind == "MLP":
        c.update(a1=n, d1=n)
    elif s.kind == "UP":
        c.update(a1=n, d1=n // 2, a2=n // 2, g1=n // 2, d2=n // 2, a3=n // 2, g2=n // 2)
    elif s.kind == "GLU":
        c.update(a1=n // 2, d1=n // 2, d2=n // 2, a2=n // 2, g1=n // 2, a3=KT, sq=KT)
    if s.ada is not None:
        c.update(ada=n, mod=n // 4)
    return c


def make_plan():
    stages = [
        Stage("ada_first", "ADA", 0),
        Stage("qk0", "QK", 16, tok=TOK, ada=(0, 16)),
        Stage("v0", "V", 8, tok=TOK, ada=(0, 32)),
        Stage("wo0", "RES", 8, tok=TOK, ada=(0, 40), norm=True, gate=(0, 2)),
        Stage("up0a", "MLP", HALF, tok=TOK, ada=(1, 0)),
        Stage("down0a", "RES", 8, units=2, tok=TOK, ada=(1, 16), gate=(0, 5)),
        Stage("up0b", "MLP", HALF, tok=TOK, ada=(1, 24)),
        Stage("down0b", "RES", 8, units=2, tok=TOK, ada=(1, 40), norm=True, gate=(0, 5)),
        Stage("q1", "QK", 8),
        Stage("k1", "QK", 2, tok=TOK),
        Stage("v1", "V", 2, tok=TOK),
        Stage("wo1", "RES", 8, norm=True, gate=(1, 2)),
        Stage("up1a", "MLP", HALF),
        Stage("down1a", "RES", 8, units=2, gate=(1, 5)),
        Stage("up1b", "MLP", HALF),
        Stage("down1b", "RES", 8, units=2, norm=True, gate=(1, 5)),
        Stage("win", "IN", 8),
        Stage("glu", "GLU", 16),
        Stage("fup0", "UP", 2 * FT),
        Stage("fdown0", "RES", 8, units=3, norm=True),
        Stage("k2", "QK", 8),
        Stage("v2", "V", 8),
        Stage("q2", "QK", 8),
        Stage("wo2", "RES", 8, norm=True),
        Stage("fup1", "UP", 2 * FT),
        Stage("fdown1", "RES", 8, units=3),
    ]
    total = {}
    tile0 = unit0 = 0
    for s in stages:
        s.base = dict(total)
        s.tile0, s.unit0 = tile0, unit0
        inc = increments(s)
        if s.name == "ada_first":
            inc = {"ada": 16, "mod": 4, "sq": KT}
        for k, v in inc.items():
            total[k] = total.get(k, 0) + v
        tile0 += s.tiles
        unit0 += s.tiles * s.units
    return {s.name: s for s in stages}, total


VEC = {}
_at = 0
for _name, _n in [("gqk0", 16), ("gqk1", 10), ("gqk2", 16), ("g_mix", 32), ("g_mlp", 32), ("a_norm", 8), ("kv_norm", 8),
                  ("b_norm", 8), ("ffn_norm", 16), ("a_d", 8), ("conv_w", 2 * 3 * FT), ("conv_b", 2 * FT),
                  ("sink", 16), ("c", 16)]:
    VEC[_name] = (_at, _n)
    _at += _n
N_VEC = _at
CON = {}
_at = 0
for _name, _n in [("ident", P), ("ones", P), ("block", P), ("perm", P), ("ntri", P), ("nones", P), ("causal", 384),
                  ("causal_neg", 384), ("window", 512), ("cos", SEQ), ("sin", SEQ)]:
    CON[_name] = (_at, _n)
    _at += _n
N_CON = _at


def program(nc, weights, ada_w, ada_b, x_t, vecs, cons, bias_na, ssm_in, ssm_bc, scratch, out):
    ST, TOTAL = make_plan()
    n_units = weights.shape[0]
    u_dram, y_dram, bat_dram, ca_dram, toep_dram, rot_dram = scratch

    ctx = ExitStack()
    with ctx:
        base = (nc.sbuf_base + 63) // 64 * 64
        cursor = [base]

        def place(name, shape, dt=F32, at=None):
            size = int(np.prod(shape[1:])) * 4
            off = cursor[0] if at is None else at
            if at is None:
                cursor[0] += (size + 31) // 32 * 32
            return nc.alloc_sbuf_tensor_at(name, shape, dt, offset=off)

        raw = place("raw", [P, RING, UNIT])
        split_at = cursor[0]
        w_hi = place("w_hi", [P, RING, UNIT], F32R)
        w_lo = place("w_lo", [P, RING, UNIT], F32R)
        ada_at = cursor[0]
        ada_raw = place("ada_raw", [P, RING, UNIT])
        h = place("h", [P, KT, TOK])
        big = cursor[0]
        cursor[0] += 64 * 1024
        u_at = cursor[0]
        u_hi = place("u_hi", [P, KT, TOK], F32R)
        u_lo = place("u_lo", [P, KT, TOK], F32R)
        con = place("con", [P, N_CON])
        vec = place("vec", [P, N_VEC])
        adab = place("adab", [P, 2, N_ADA, 2])
        mod = place("mod", [P, 2, N_ADA, 2])
        gain = place("gain", [P, 2, 2, KT, 2])
        silu = place("silu", [P, KT, 2])
        sq = place("sq", [P, 2, TOK])
        rs = place("rs", [P, 2, TOK])
        rsn = place("rsn", [P, TOK])
        ssum = place("ssum", [P, TOK])
        tmp = place("tmp", [P, 2, TOK])
        half_eps = place("half_eps", [P, 1])
        two = place("two", [P, 1])

        hid_hi = place("hid_hi", [P, HALF, TOK], F32R, at=big)
        hid_lo = place("hid_lo", [P, HALF, TOK], F32R, at=big + 32768)
        qk0 = place("qk0", [P, 16, TOK], at=big)
        val0 = place("val0", [P, 4, D], at=big + 32768)
        q1 = place("q1", [P, 8, SEQ], at=big)
        k1 = place("k1", [P, 2, TOK], at=big + 8192)
        val1 = place("val1", [P, 4, 256], at=big + 32768)
        k2 = place("k2", [P, 8, SEQ], at=big)
        q2 = place("q2", [P, 8, SEQ], at=big + 8192)
        val2 = place("val2", [P, 2, D], at=big + 32768)
        at_ = big + 49152
        s_sb = place("s_sb", [P, 2, 256], at=at_)
        prob = place("prob", [P, 2, TOK], at=at_ + 2048)
        prob_t = place("prob_t", [P, 2, TOK], at=at_ + 6144)
        bias_sb = place("bias_sb", [P, 3, 256], at=at_ + 10240)
        o_pair = place("o_pair", [P, 2, P], at=at_ + 13312)
        stat = place("stat", [P, 4, 8], at=at_ + 14336)
        sb_r = place("sb_r", [P, 2, 384], at=big + 16384)
        sb_n = place("sb_n", [P, 2, 384], at=big + 16384 + 3072)
        sb_e = place("sb_e", [P, 2, 384], at=big + 16384 + 6144)
        sb_w = place("sb_w", [P, 2, 384], at=big + 16384 + 9216)
        f_hi = place("f_hi", [P, FT, SEQ], F32R, at=big)
        f_lo = place("f_lo", [P, FT, SEQ], F32R, at=big + FT * 1024)
        fx = big + 2 * FT * 1024
        f_val = place("f_val", [P, 2, SEQ], at=fx)
        f_gate = place("f_gate", [P, 2, SEQ + 2], at=fx + 2048)
        f_c = place("f_c", [P, 2, SEQ], at=fx + 4128)
        f_e = place("f_e", [P, 2, SEQ], at=fx + 6176)
        f_h = place("f_h", [P, 2, SEQ], at=fx + 8224)
        f_y = place("f_y", [P, 2, SEQ], at=fx + 10272)
        f_t = place("f_t", [P, 2, SEQ], at=fx + 12320)

        ba = place("ba", [P, PAIRS, 2, CH, SSM_H], at=big)
        ca = place("ca", [P, PAIRS, 2, POW, SSM_H], at=big + 32768)
        c_at = big + 32768 + 36864
        bat = place("bat", [P, 2, QJ, P], at=c_at)
        kern = place("kern", [SSM_H, 2 * QJ, P], at=c_at + 8192)
        ktmp = place("ktmp", [P, QJ, CH, SSM_H], at=c_at + 16384)
        ctmp = place("ctmp", [P, QJ, POW, SSM_H], at=c_at + 20480)
        rot0 = place("rot0", [P, 3, PAIRS, NCH], at=split_at)
        bbar = place("bbar", [P, 2, PAIRS, SSM_H], at=split_at + 12288)
        bc = place("bc", [P, 4, PAIRS, SSM_H], at=split_at + 16384)
        pw = place("pw", [P, 3, 2, POW, PAIRS], at=split_at + 24576)
        assert 3 * 2 * POW * PAIRS * 4 <= 8192
        sv = place("sv", [P, 24, PAIRS], at=c_at + 25088)
        assert cursor[0] <= nc.sbuf_usable_end, cursor[0] - nc.sbuf_usable_end

        s_bat = place("s_bat", [P, 2, QJ, 2, P], at=big)
        s_ca = place("s_ca", [P, 2, QJ, 2, P], at=big + 16384)
        s_toep = place("s_toep", [P, 2, 2 * QJ, P], at=big + 32768)
        u_sc = place("u_sc", [P, KT, CH, NCH], at=big + 49152)
        y_g = place("y_g", [P, GROUPS, NCH], at=big + 57344)
        u_g = place("u_g", [P, GROUPS, NCH], at=u_at)
        x_mod = place("x_mod", [P, 2, 2, QJ, NCH], at=u_at + 8192)
        x_tmp = place("x_tmp", [P, 2, QJ, NCH], at=u_at + 12288)
        g_st = place("g_st", [P, 2, 2, QJ, NCH], at=u_at + 16384)
        h_st = place("h_st", [P, 2, 2, QJ, NCH], at=u_at + 20480)
        g_tmp = place("g_tmp", [P, 2, QJ, NCH], at=u_at + 24576)
        rot = place("rot", [P, 3, PAIRS, NCH], at=ada_at)
        y2 = place("y2", [P, KT, CH, NCH], at=big)
        ge = place("ge", [P, 5, 2, CH, NCH], at=big + 8192)

        psum = [ctx.enter_context(nc.psum_tensor(f"bank{i}", [P, 512], F32)) for i in range(8)]
        TILE, SS, SS2, ADA_BANK, O_BANK = psum[0:4], psum[4], psum[5], psum[6], psum[7]

        def C(name, n=None):
            a, m = CON[name]
            return con[:, a:a + (n or m)]

        def VC(name, i, parts=slice(0, P)):
            return vec[parts, bass.ds(VEC[name][0] + i, 1)]

        def sem(name):
            return ctx.enter_context(nc.semaphore(name))

        raw_in = [sem(f"raw_in{i}") for i in range(RING)]
        ada_in = [sem(f"ada_in{i}") for i in range(RING)]
        small_in = sem("small_in")
        ssm_par_in = sem("ssm_par_in")
        S = {
            "hi": sem("unit_hi"),
            "lo": sem("unit_lo"),
            "unit": sem("unit_done"),
            "ada": sem("ada_done"),
            "mod": sem("mod_done"),
            "a1": sem("act_first"), "a2": sem("act_second"), "a3": sem("act_third"),
            "d1": sem("dve_first"), "d2": sem("dve_second"), "d3": sem("dve_sum"),
            "p2": sem("pe_heads"),
            "sq": sem("pe_rows"),
            "g1": sem("pool_newton"),
            "g2": sem("pool_lower"),
        }
        act_chain, dve_chain, pool_chain = sem("act_chain"), sem("dve_chain"), sem("pool_chain")
        const_set = sem("const_set")
        silu_e, silu_d = sem("silu_e"), sem("silu_d")
        ss0, x_in, pre_cout, pre_zero = sem("ss0"), sem("x_in"), sem("pre_ca_out"), sem("pre_zero")
        gain_done = sem("gain_done")
        n_v, n_rs, n_t, n_hi, n_lo = sem("norm_mean"), sem("norm_root"), sem("norm_scaled"), sem("norm_hi"), sem("norm_lo")
        att_s, att_m, att_p, att_t, att_e, att_o, att_n, att_x, att_h, att_l = (sem("att_" + c) for c in (
            "scores", "max", "probs", "transposed", "probs_t", "out", "normalised", "out_t", "out_hi", "out_lo"))
        bias_in = [sem(f"bias_in{i}") for i in range(3)]
        rope_p, rope_d = sem("rope_rotated"), sem("rope_done")
        sb_s, sb_d1, sb_a1, sb_d2, sb_c, sb_d3, sb_a2, sb_o, sb_h, sb_l = (sem("sb_" + c) for c in (
            "scores", "neg_abs", "log", "masked", "sums", "exponent", "weights", "out", "out_hi", "out_lo"))
        pre_e, pre_v, pre_b, pre_c, pre_t, pre_ta, pre_k, pre_ka, pre_kout = (sem("pre_" + c) for c in (
            "exp", "small", "ba", "ca", "transposed", "bat", "kernel", "kern", "kern_out"))
        pre_out = [sem("pre_bat_out_re"), sem("pre_bat_out_im")]
        u_out, u_in, rot_in = sem("u_out"), sem("u_in"), sem("rot_in")
        bat_in, ssm_in_s = [sem("bat_in0"), sem("bat_in1")], [sem("tab_in0"), sem("tab_in1")]
        ssm_x, ssm_h, ssm_y, ssm_ya, y_out, y_in = sem("ssm_x"), sem("ssm_h"), sem("ssm_y"), sem("ssm_ya"), sem("y_out"), sem("y_in")
        ssm_free = sem("ssm_free")
        ge2, ge3, ge_n, ge4, ge5, ge6 = (sem("gelu_" + c) for c in (
            "argument", "reciprocal", "newton", "product", "out_hi", "out_lo"))
        h_out = sem("h_out")

        block = ctx.enter_context(nc.Block())

        def value(name, s, n):
            return n + (CREDIT + s.base.get(name, 0))

        def stage_end(eng, s, names):
            inc = increments(s)
            for n in names:
                if n in inc:
                    eng.wait_ge(S[n], CREDIT + s.base.get(n, 0) + inc[n])

        class Chain:

            def __init__(self, eng, s):
                self.eng, self.s, self.n, self.expr = eng, s, 0, 0

            def link(self, ins):
                self.n += 1
                ins.then_inc(self.s, 1)
                self.eng.wait_ge(self.s, self.expr + self.n)

        @contextmanager
        def repeat(eng, n, chain=None, per=0):
            if n == 1:
                yield 0
                return
            with eng.Fori(0, n) as i:
                if chain is not None:
                    start = chain.n
                    chain.expr = i * per
                yield i
                if chain is not None:
                    assert chain.n - start == per, (chain.n - start, per)
                    chain.expr = 0
            if chain is not None:
                chain.n = start + per * n

        NORM_TOK = {"mix0": TOK, "mlp0": TOK, "mix1": TOK}
        NORM_AFTER = {"mlp0": "wo0", "mix1": "down0b", "mlp1": "wo1", "a": "down1b", "ffn0": "glu", "kv": "fdown0", "ffn1": "wo2"}
        NORM_BEFORE = {"qk0": 0, "up0a": 1, "q1": 2, "up1a": 3, "win": 4, "fup0": 5, "k2": 6, "q2": 7, "fup1": 8}
        HIDDEN = {"down0a": ("up0a", "d1"), "down0b": ("up0b", "d1"), "down1a": ("up1a", "d1"), "down1b": ("up1b", "d1"),
                  "fdown0": ("fup0", "g2"), "fdown1": ("fup1", "g2")}
        MODS_NEEDED = {"mix0": 4, "mlp0": 10, "mix1": 16, "mlp1": 22}
        VAL = {"v0": val0, "v1": val1, "v2": val2}
        QK_DST = {"qk0": qk0, "q1": q1, "k1": k1, "k2": k2, "q2": q2}
        QK_GAIN = {"qk0": ("gqk0", 0), "q1": ("gqk1", 0), "k1": ("gqk1", 8), "k2": ("gqk2", 0), "q2": ("gqk2", 8)}

        def row_sums(s):
            return bool(s.more.get("norm"))

        def ge_flat(n, k):
            return ge[:, n, k % 2, :, :].rearrange("p s c -> p (s c)")

        def mod_norm(name):
            return (int(name[3]), int(name[:3] == "mlp")) if name in MODS_NEEDED else None

        def norm_gain(name, kt, hf):
            if mod_norm(name):
                layer, which = mod_norm(name)
                return gain[:, layer, which, kt, hf:hf + 1]
            return {"a": VC("a_norm", kt), "ffn0": VC("ffn_norm", kt), "kv": VC("kv_norm", kt), "b": VC("b_norm", kt),
                    "ffn1": VC("ffn_norm", KT + kt)}[name]

        def shift(name, kt, hf):
            if not mod_norm(name):
                return None
            layer, which = mod_norm(name)
            return mod[:, layer, 24 * which + kt, hf:hf + 1]

        ATT0, ATT1 = [], []
        for ctx_side in range(2):
            for qt in range(2):
                for hd in range(HEADS):
                    hb, hp = (hd % 2) * HD, hd // 2
                    at0 = ctx_side * SEQ + qt * P
                    keys = TOK if ctx_side == 0 else SEQ
                    ATT0.append((qk0[hb:hb + HD, hp, at0:at0 + P], qk0[hb:hb + HD, KT + hp, TOK - keys:TOK],
                                 [val0[:, t, hp * P:(hp + 1) * P] for t in range((TOK - keys) // P, 4)], keys, TOK - keys,
                                 (hp, slice(at0, at0 + P)), ("ctx",) if ctx_side else ("na", qt * HEADS + hd)))
        for qt in range(2):
            for pos in range(HEADS):
                hb, hp = (pos % 2) * HD, pos // 2
                ATT1.append((q1[hb:hb + HD, hp, qt * P:(qt + 1) * P], k1[hb:hb + HD, hp // 4, :],
                             [val1[:, t, (hp // 4) * P:(hp // 4 + 1) * P] for t in range(4)], TOK, 0,
                             (hp, slice(qt * P, (qt + 1) * P)), ("swa", qt, pos)))

        @block.sync
        def _(sp):
            sp.dma_start(vec[:, :], vecs).then_inc(small_in, 16)
            sp.dma_start(h[:, :, :], x_t).then_inc(x_in, 16)
            sp.dma_start(con[:, :], cons).then_inc(small_in, 16)
            sp.dma_start(adab[:, :, :, :], ada_b).then_inc(small_in, 16)

            def load_ada(index, slot, turn):
                sp.wait_ge(S["ada"], index + 1)
                sp.dma_start(ada_raw[:, slot, :], ada_w[index]).then_inc(ada_in[slot], 16)

            def load_unit(index, slot):
                sp.wait_ge(S["lo"], index + 1)
                sp.dma_start(raw[:, slot, :], weights[index]).then_inc(raw_in[slot], 16)

            with repeat(sp, 4) as i:
                for k in range(4):
                    load_ada(i * 4 + k, k, i)
            for s in ST.values():
                if not s.tiles:
                    continue
                body = min(4, s.tiles)
                with repeat(sp, s.tiles // body) as i:
                    for jj in range(body):
                        for k in range(s.units):
                            n = jj * s.units + k
                            load_unit(i * (body * s.units) + (s.unit0 + n), (s.unit0 + n) % RING)
                        if s.ada is not None:
                            load_ada(i * 4 + (s.base["ada"] + jj), jj, i)
            last = ST["fdown1"]
            for m in range(KT):
                sp.wait_ge(S["d1"], value("d1", last, m + 1))
                sp.dma_start(out[:, m, :], h[:, m, 0:SEQ]).then_inc(h_out, 16)
            sp.wait_ge(h_out, 16 * KT)

        @block.tensor
        def _(pe):
            pe.nop().then_inc(S["unit"], CREDIT)
            pe.nop().then_inc(S["ada"], CREDIT)
            pe.nop().then_inc(S["p2"], CREDIT)
            pe.nop().then_inc(S["sq"], CREDIT)

            def ada_unit(slot, landed, col):
                pe.wait_ge(ada_in[slot], landed)
                for kt in range(KT):
                    mm = pe.matmul(ADA_BANK[:, bass.ds(2 * col, 2)], ada_raw[:, slot, kt * P:(kt + 1) * P],
                                   silu[:, kt, :], start=(kt == 0), stop=(kt == KT - 1))
                mm.then_inc(S["ada"], 1)

            OPER = {}
            for s in ST.values():
                OPER[s.name] = (u_hi, u_lo)
            for n in ("down0a", "down0b", "down1a", "down1b"):
                OPER[n] = (hid_hi, hid_lo)
            for n in ("fdown0", "fdown1"):
                OPER[n] = (f_hi, f_lo)
            SUM_BANKS = (SS, SS2)

            def gemm_tile(s, i, jj, body):
                hi, lo = OPER[s.name]
                bank = TILE[(s.tile0 + jj) % RING]
                j = i * body + jj
                if s.kind == "V":
                    value_tile(s, i, jj, body)
                    return
                for n in {"QK": ("a1", "d1"), "IN": ("a1",), "RES": ("d1",), "MLP": ("a1",), "UP": ("a1",),
                          "GLU": ()}[s.kind]:
                    pe.wait_ge(S[n], value(n, s, j - 3))
                if s.kind == "GLU":
                    n = ("a1", "d2")[jj % 2]
                    pe.wait_ge(S[n], value(n, s, i * 2 + (jj // 2 - 1)))
                total = {2: 16, 3: FT}.get(s.units, KT)
                for k in range(s.units):
                    n = jj * s.units + k
                    slot = (s.unit0 + n) % RING
                    pe.wait_ge(S["lo"], i * (body * s.units) + (CREDIT + s.unit0 + n + 1))
                    here = min(KT, total - k * KT)
                    for t in range(here):
                        kt = k * KT + t
                        first, final = kt == 0, kt == total - 1
                        if jj == 0 and s.name in NORM_BEFORE:
                            pe.wait_ge(n_lo, 8 * NORM_BEFORE[s.name] + kt + 1)
                        if jj == 0 and s.name == "glu":
                            pe.wait_ge(ge6, kt + 1)
                        if jj == 0 and s.name in HIDDEN:
                            made, n = HIDDEN[s.name]
                            pe.wait_ge(S[n], value(n, ST[made], kt + 1))
                        wh, wl = w_hi[:, slot, t * P:(t + 1) * P], w_lo[:, slot, t * P:(t + 1) * P]
                        dst = bank[:, 0:s.tok]
                        pe.matmul(dst, wh, hi[:, kt, 0:s.tok], start=first, stop=False)
                        pe.matmul(dst, wh, lo[:, kt, 0:s.tok], start=False, stop=False)
                        mm = pe.matmul(dst, wl, hi[:, kt, 0:s.tok], start=False, stop=final)
                    mm.then_inc(S["unit"], 1)

            def value_tile(s, i, jj, body):
                hi, lo = OPER[s.name]
                if jj % 2 == 0:
                    pe.wait_ge(S["a1"], value("a1", s, i * (body // 2) + (jj // 2 - 1)))
                slot = (s.unit0 + jj) % RING
                pe.wait_ge(S["lo"], i * body + (CREDIT + s.unit0 + jj + 1))
                for t in range(KT // 2):
                    kt = jj % 2 * (KT // 2) + t
                    first, final = kt == 0, kt == KT - 1
                    wh, wl = (w[:, slot, t * VW:(t + 1) * VW] for w in (w_hi, w_lo))
                    for tt in range(s.tok // P):
                        xs = slice(tt * P, (tt + 1) * P)
                        dst = TILE[jj // 2 % 2 * 2 + tt // 2][:, tt % 2 * VW:(tt % 2 + 1) * VW]
                        pe.matmul(dst, hi[:, kt, xs], wh, start=first and tt % 2 == 0, stop=False, skip_group_check=True)
                        pe.matmul(dst, lo[:, kt, xs], wh, start=False, stop=False, skip_group_check=True)
                        mm = pe.matmul(dst, hi[:, kt, xs], wl, start=False, stop=final, skip_group_check=True)
                mm.then_inc(S["unit"], 1)

            def sum_tile(s, i, jj, body):
                j = i * body + jj
                if s.kind == "QK":
                    pe.wait_ge(S["a1"], value("a1", s, j + 1))
                    pe.wait_ge(S["a2"], value("a2", s, j - 1))
                    pe.matmul(SUM_BANKS[(s.tile0 + jj) % 2][:, 0:s.tok], C("block"), sq[:, (s.tile0 + jj) % 2, 0:s.tok],
                              start=True, stop=True).then_inc(S["p2"], 1)
                else:
                    pe.wait_ge(S["a1"], value("a1", s, i * body + (jj + 1)))
                    if jj == 0:
                        pe.wait_ge(S["d3"], value("d3", s, i * 1))
                    pe.matmul(SS[:, 0:s.tok], C("ones"), sq[:, jj % 2, 0:s.tok], start=(jj == 0),
                              stop=(jj == body - 1)).then_inc(S["sq"], 1)

            def gemm(name):
                s = ST[name]
                body = min(4, s.tiles)
                sums = s.kind == "QK" or row_sums(s)
                with repeat(pe, s.tiles // body) as i:
                    for jj in range(body):
                        gemm_tile(s, i, jj, body)
                        if s.ada is not None and jj == 0:
                            pe.wait_ge(S["mod"], i * 1 + (CREDIT + s.base["mod"]))
                        if s.ada is not None:
                            ada_unit(jj, i * 16 + 16 * (s.base["ada"] // 4 + 1), jj)
                        if sums and jj:
                            sum_tile(s, i, jj - 1, body)
                    if sums:
                        sum_tile(s, i, body - 1, body)

            def drained(name):
                stage_end(pe, ST[name], ("a1", "d1", "a2", "d2", "a3", "d3"))

            def copied(name):
                stage_end(pe, ST[name], ("a1",))

            pe.wait_ge(small_in, 48)
            for kt in range(KT):
                pe.wait_ge(ss0, kt + 1)
                pe.matmul(SS[:, :], C("ones"), sq[:, kt % 2, :], start=(kt == 0), stop=(kt == KT - 1)).then_inc(S["sq"], 1)
            pe.wait_ge(silu_d, 1)
            with repeat(pe, 2) as i:
                for k in range(4):
                    ada_unit(k, i * 16 + 16, i * 4 + k)

            for q in range(NQ):
                pe.wait_ge(pre_b, q + 1)
                for ri in range(2):
                    n = q * 2 + ri
                    for hf in range(2):
                        if n >= 1:
                            pe.wait_ge(pre_ta, 2 * (n - 1) + hf + 1)
                        for t in range(4):
                            j = q * QJ + hf * 4 + t
                            mm = pe.transpose(TILE[hf][:, t * P:(t + 1) * P],
                                              ba[:, j, ri, :, :].rearrange("p s h -> p (s h)"), C("ident"))
                        mm.then_inc(pre_t, 1)
                pe.wait_ge(pre_c, q + 1)
                for n in range(4 * q, 4 * q + 4):
                    if n >= 2:
                        pe.wait_ge(pre_ka, n - 1)
                    for t in range(4):
                        j, hb = 4 * (n // 2) + t, (n % 2) * 64
                        for ri in range(2):
                            mm = pe.matmul(TILE[2 + n % 2][0:SSM_H, t * P:(t + 1) * P], bbar[hb:hb + 64, ri, j, :],
                                           ca[hb:hb + 64, j, ri, 0:CH, :].rearrange("p s h -> p (s h)"),
                                           start=(ri == 0), stop=(ri == 1))
                    mm.then_inc(pre_k, 1)
                if q < 2:
                    for k in range(4):
                        ada_unit(k, 16 * (q + 3), 8 + 4 * q + k)

            def attention(units, kbase):
                n_u = len(units)
                for n in range(n_u + 5):
                    if n < n_u:
                        q_ap, k_ap, _, keys, s_off = units[n][:5]
                        if n + kbase >= 3:
                            pe.wait_ge(att_p, n + kbase - 2)
                        pe.matmul(psum[(n + kbase) % 3][:, s_off:s_off + keys], q_ap, k_ap, start=True, stop=True).then_inc(att_s, 1)
                    m = n - 1
                    if 0 <= m < n_u:
                        keys = units[m][3]
                        g = m + kbase
                        pe.wait_ge(att_p, g + 1)
                        if g >= 2:
                            pe.wait_ge(att_e, g - 1)
                        for t in range(keys // P):
                            mm = pe.transpose(psum[3 + g % 2][:, t * P:(t + 1) * P], prob[:, g % 2, t * P:(t + 1) * P], C("ident"))
                        mm.then_inc(att_t, 1)
                    m = n - 2
                    if 0 <= m < n_u:
                        v_aps, keys = units[m][2], units[m][3]
                        g = m + kbase
                        pe.wait_ge(att_e, g + 1)
                        if g >= 2:
                            pe.wait_ge(att_n, g - 1)
                        for t in range(keys // P):
                            mm = pe.matmul((psum[5], psum[7])[g % 2][:, 0:P], prob_t[:, g % 2, t * P:(t + 1) * P], v_aps[t],
                                           start=(t == 0), stop=(t == keys // P - 1))
                        mm.then_inc(att_o, 1)
                    m = n - 4
                    if 0 <= m < n_u and m % 2 == 1:
                        pr = (m + kbase) // 2
                        pe.wait_ge(att_n, m + kbase + 1)
                        if pr >= 1:
                            pe.wait_ge(att_l, pr)
                        pe.transpose(psum[6][:, 0:P], o_pair[:, pr % 2, :], C("ident")).then_inc(att_x, 1)

            gemm("qk0")
            stage_end(pe, ST["qk0"], ("a1", "d1"))
            gemm("v0")
            drained("v0")
            drained("qk0")
            pe.wait_ge(S["mod"], CREDIT + ST["wo0"].base["mod"])
            attention(ATT0, 0)
            pe.wait_ge(att_l, 32)
            gemm("wo0")
            drained("wo0")
            gemm("up0a"); copied("up0a"); gemm("down0a"); drained("down0a")
            gemm("up0b"); copied("up0b"); gemm("down0b"); drained("down0b")
            gemm("q1"); drained("q1"); gemm("k1"); drained("k1"); gemm("v1"); drained("v1")
            for m in range(10):
                dst = q1[:, m, :] if m < 8 else k1[:, m - 8, 0:SEQ]
                if m >= 2:
                    pe.wait_ge(rope_d, m - 1)
                pe.matmul(SUM_BANKS[m % 2][:, 0:SEQ], C("perm"), dst, start=True, stop=True).then_inc(rope_p, 1)
            pe.wait_ge(rope_d, 10)
            attention(ATT1, 64)
            pe.wait_ge(att_l, 48)
            gemm("wo1"); drained("wo1")
            gemm("up1a"); copied("up1a"); gemm("down1a"); drained("down1a")
            gemm("up1b"); copied("up1b"); gemm("down1b"); drained("down1b")
            gemm("win"); drained("win")

            pe.wait_ge(u_in, 16 * CH)
            def ssm_states(q):
                pe.wait_ge(bat_in[q % 2], 16 * (q // 2 + 1))
                if q >= 2:
                    pe.wait_ge(ssm_h, q - 1)
                for jj in range(QJ):
                    for hf in range(2):
                        g = (q * QJ + jj) * 2 + hf
                        for ri in range(2):
                            at = (jj * 2 + ri) * NCH
                            mm = pe.matmul(psum[q % 2][hf * 64:hf * 64 + 64, at:at + NCH],
                                           s_bat[:, q % 2, jj, ri, hf * 64:hf * 64 + 64], u_g[:, g, :], start=True, stop=True,
                                           skip_group_check=True)
                mm.then_inc(ssm_x, 1)

            def ssm_outputs(q):
                pe.wait_ge(ssm_h, q + 1)
                pe.wait_ge(ssm_in_s[q % 2], 32 * (q // 2 + 1))
                if q >= 2:
                    pe.wait_ge(ssm_ya, q - 1)
                for jj in range(QJ):
                    for hf in range(2):
                        gl = jj * 2 + hf
                        g = q * QJ * 2 + gl
                        hb = hf * 64
                        dst = psum[(2, 6)[q % 2] + hf][:, jj * NCH:(jj + 1) * NCH]
                        pe.matmul(dst, s_toep[:, q % 2, gl, :], u_g[:, g, :], start=True, stop=False)
                        pe.matmul(dst, s_ca[hb:hb + 64, q % 2, jj, 0, :], h_st[hb:hb + 64, q % 2, 0, jj, :], start=False, stop=False)
                        mm = pe.matmul(dst, s_ca[hb:hb + 64, q % 2, jj, 1, :], h_st[hb:hb + 64, q % 2, 1, jj, :],
                                       start=False, stop=True)
                mm.then_inc(ssm_y, 1)

            ssm_states(0)
            for q in range(NQ):
                if q + 1 < NQ:
                    ssm_states(q + 1)
                ssm_outputs(q)
            pe.wait_ge(ssm_ya, NQ)
            gemm("glu")
            for kt in range(KT):
                pe.wait_ge(S["a3"], value("a3", ST["glu"], kt + 1))
                pe.matmul(SS[:, 0:SEQ], C("ones"), sq[:, kt % 2, 0:SEQ], start=(kt == 0), stop=(kt == KT - 1)).then_inc(S["sq"], 1)
            drained("glu")
            gemm("fup0"); copied("fup0"); gemm("fdown0"); drained("fdown0")
            gemm("k2"); drained("k2"); gemm("v2"); drained("v2")
            gemm("q2"); drained("q2")

            def sb_scores(n):
                hb = (n % 2) * 64
                hp = n // 2
                if n >= 3:
                    pe.wait_ge(sb_d3, n - 2)
                dst = psum[n % 3]
                pe.matmul(dst[:, 0:SEQ], k2[hb:hb + 64, hp, 0:P], q2[hb:hb + 64, hp, :], start=True, stop=False, skip_group_check=True)
                pe.matmul(dst[:, SEQ:SEQ + P], k2[hb:hb + 64, hp, P:SEQ], q2[hb:hb + 64, hp, P:SEQ],
                          start=False, stop=False, skip_group_check=True).then_inc(sb_s, 1)

            def sb_sums(n):
                pe.wait_ge(sb_d2, n + 1)
                dst = psum[n % 3]
                m = sb_r[:, n % 2, :]
                pe.matmul(dst[:, 0:384], C("ntri"), m[:, 0:384], start=False, stop=False, skip_group_check=True)
                pe.matmul(dst[:, P:SEQ], C("nones"), m[:, SEQ:SEQ + P], start=False, stop=True,
                          skip_group_check=True).then_inc(sb_c, 1)

            def sb_values(n):
                pe.wait_ge(sb_a2, n + 1)
                hb = (n % 2) * 64
                pr = n // 2
                if n % 2 == 0 and pr >= 2:
                    pe.wait_ge(sb_l, pr - 1)
                dst = psum[4 + pr % 2][hb:hb + 64, 0:SEQ]
                pe.matmul(dst, val2[:, 0, n * HD:(n + 1) * HD], sb_w[:, n % 2, 0:SEQ], start=True, stop=False, skip_group_check=True)
                pe.matmul(dst[:, P:SEQ], val2[:, 1, n * HD:(n + 1) * HD], sb_w[:, n % 2, SEQ:384],
                          start=False, stop=True, skip_group_check=True).then_inc(sb_o, 1)

            for n in range(HEADS + 2):
                if n < HEADS:
                    sb_scores(n)
                if 1 <= n <= HEADS:
                    sb_sums(n - 1)
                if 2 <= n:
                    sb_values(n - 2)
            pe.wait_ge(sb_l, 8)
            gemm("wo2"); drained("wo2")
            gemm("fup1"); copied("fup1"); gemm("fdown1")

        @block.scalar
        def _(act):
            act.preload_act_table_set("natural_log_exp_and_others")
            for n in ("hi", "a1", "a2", "a3"):
                act.nop().then_inc(S[n], CREDIT)
            chain = Chain(act, act_chain)
            A = act.activation

            def split_unit(s, i, n, per):
                g = s.unit0 + n + 3
                if g >= n_units:
                    return
                slot = g % RING
                act.wait_ge(raw_in[slot], i * (16 * per // RING) + 16 * (g // RING + 1))
                act.wait_ge(S["unit"], i * per + (g + 1))
                A(w_hi[:, slot, :], raw[:, slot, :], ACT.Copy).then_inc(S["hi"], 1)

            def root(dst, src):
                chain.link(A(dst, src, ACT.Ln, scale=-2.0))
                return A(dst, dst, ACT.Exp, scale=-0.5)

            def tile(s, i, jj, body, first=False):
                j = i * body + jj
                bank = TILE[(s.tile0 + jj) % RING]
                n_done = i * (body * s.units) + (CREDIT + s.unit0 + (jj + 1) * s.units)
                b2 = (s.tile0 + jj) % 2
                if s.kind == "QK":
                    act.wait_ge(S["unit"], n_done)
                    act.wait_ge(S["p2"], value("p2", s, j - 1))
                    act.wait_ge(S["d2"], value("d2", s, j - 1))
                    A(sq[:, b2, 0:s.tok], bank[:, 0:s.tok], ACT.Square).then_inc(S["a1"], 1)
                    if jj:
                        qk_root(s, i, jj - 1, body)
                elif s.kind == "V":
                    if jj % 2:
                        act.wait_ge(S["unit"], n_done)
                        cols = bass.ds(i * (body // 2 * VW) + jj // 2 * VW, VW)
                        for b in range(s.tok // SEQ):
                            last = A(VAL[s.name][:, 2 * b:2 * b + 2, cols],
                                     TILE[jj // 2 % 2 * 2 + b][:, :].rearrange("p (t c) -> p t c", c=VW), ACT.Copy)
                        last.then_inc(S["a1"], 1)
                elif s.kind == "IN":
                    act.wait_ge(S["unit"], n_done)
                    A(u_sc[:, bass.ds(j, 1), :, :].rearrange("p a s c -> p (a s) c"),
                      bank[:, 0:SEQ].rearrange("p (c s) -> p s c", s=CH), ACT.Copy).then_inc(S["a1"], 1)
                elif s.kind == "RES":
                    if s.more.get("norm"):
                        act.wait_ge(S["d1"], value("d1", s, j + 1))
                        act.wait_ge(S["sq"], value("sq", s, j - 1))
                        A(sq[:, jj % 2, 0:s.tok], h[:, bass.ds(j, 1), 0:s.tok].rearrange("p a t -> p (a t)"),
                          ACT.Square).then_inc(S["a1"], 1)
                elif s.kind == "MLP":
                    act.wait_ge(S["unit"], n_done)
                    act.wait_ge(S["d1"], value("d1", s, j - 1))
                    act.wait_ge(S["a1"], value("a1", s, j - 1))
                    chain.link(A(rs[:, b2, 0:s.tok], bank[:, 0:s.tok], ACT.Relu))
                    A(hid_hi[:, bass.ds(j, 1), 0:s.tok].rearrange("p a t -> p (a t)"), rs[:, b2, 0:s.tok],
                      ACT.Square).then_inc(S["a1"], 1)
                elif s.kind == "UP":
                    pb = (jj // 2) % 2
                    pair = i * 2 + jj // 2
                    if jj == 3:
                        sigmoid(s, i, 0)
                    act.wait_ge(S["unit"], n_done)
                    if jj % 2 == 0:
                        act.wait_ge(S["d2"], value("d2", s, pair - 1))
                        A(f_val[:, pb, :], bank[:, 0:SEQ], ACT.Copy).then_inc(S["a1"], 1)
                    else:
                        A(f_gate[:, pb, 2:2 + SEQ], bank[:, 0:SEQ], ACT.Copy).then_inc(S["a1"], 1)
                    if jj < 2 and not first:
                        hidden(s, i * 2 - 2 + jj, jj)
                elif s.kind == "GLU":
                    pb = (jj // 2) % 2
                    pair = i * 2 + jj // 2
                    if jj % 2 == 0:
                        act.wait_ge(S["unit"], n_done)
                        act.wait_ge(S["d1"], value("d1", s, pair - 1))
                        A(rs[:, pb, 0:SEQ], bank[:, 0:SEQ], ACT.Copy).then_inc(S["a1"], 1)
                    if jj == 2:
                        sigmoid(s, i, 0)

            def sigmoid(s, i, pb):
                e = f_e[:, pb, :] if s.kind == "UP" else tmp[:, pb, 0:SEQ]
                n = "d1" if s.kind == "UP" else "d2"
                act.wait_ge(S[n], value(n, s, i * 2 + (pb + 1)))
                chain.link(A(e, e, ACT.Exp, scale=-1.0))
                chain.link(A(f_y[:, pb, :], e, ACT.Ln, bias=C("ones")[:, 0:1]))
                A(f_y[:, pb, :], f_y[:, pb, :], ACT.Exp, scale=-1.0).then_inc(S["a2"], 1)

            def hidden(s, pair, pb):
                act.wait_ge(S["d2"], value("d2", s, pair + 1))
                A(f_hi[:, bass.ds(pair, 1), :].rearrange("p a t -> p (a t)"), f_h[:, pb, :], ACT.Copy).then_inc(S["a3"], 1)

            def qk_root(s, i, jj, body):
                j = i * body + jj
                b2 = (s.tile0 + jj) % 2
                act.wait_ge(S["p2"], value("p2", s, j + 1))
                act.wait_ge(S["d2"], value("d2", s, j - 1))
                v, y = tmp[:, b2, 0:s.tok], rs[:, b2, 0:s.tok]
                chain.link(A(v, (SS, SS2)[b2][:, 0:s.tok], ACT.Identity, bias=half_eps[:, :], scale=-0.5 * INV_HD))
                chain.link(root(y, v))
                A(sq[:, b2, 0:s.tok], y, ACT.Square).then_inc(S["a2"], 1)

            def stage(name):
                s = ST[name]
                body = min(4, s.tiles)
                per = body * s.units
                n_links = {"QK": 3 * body, "MLP": body, "UP": body, "GLU": body}.get(s.kind, 0)

                def one(i, first=False, last=False):
                    for jj in range(body):
                        for k in range(s.units):
                            n = jj * s.units + k
                            if not last:
                                split_unit(s, i, n, per)
                            elif s.unit0 + per + n + 3 < n_units:
                                split_unit_at(s.unit0 + per + n + 3)
                        tile(s, i, jj, body, first)
                    if s.kind == "QK":
                        qk_root(s, i, body - 1, body)
                    if s.kind in ("UP", "GLU"):
                        sigmoid(s, i, 1)

                if name == "fdown1":
                    one(0)
                    one(1, last=True)
                elif s.kind == "UP":
                    one(0, first=True)
                    with repeat(act, s.tiles // body - 1, chain, n_links) as i:
                        one(i + 1)
                    hidden(s, s.tiles // 2 - 2, 0)
                    hidden(s, s.tiles // 2 - 1, 1)
                else:
                    with repeat(act, s.tiles // body, chain, n_links) as i:
                        one(i)

            def split_unit_at(g):
                slot = g % RING
                act.wait_ge(raw_in[slot], 16 * (g // RING + 1))
                act.wait_ge(S["unit"], g + 1)
                A(w_hi[:, slot, :], raw[:, slot, :], ACT.Copy).then_inc(S["hi"], 1)

            act.wait_ge(small_in, 48)
            act.wait_ge(const_set, 2)
            A(silu[:, :, :], silu[:, :, :], ACT.Exp, scale=-1.0).then_inc(silu_e, 1)
            act.wait_ge(ssm_par_in, 32)
            chain.link(A(sv[:, 3, :], sv[:, 2, :], ACT.Exp))
            act.nop().then_inc(pre_e, 1)
            act.wait_ge(pre_v, 1)
            A(sv[:, 6, :], sv[:, 4, :], ACT.Exp)
            A(sv[:, 7, :], sv[:, 4, :], ACT.Exp, scale=float(CH)).then_inc(pre_e, 1)
            for kt in range(KT):
                if kt == 0:
                    act.wait_ge(x_in, 16)
                if kt >= 2:
                    act.wait_ge(S["sq"], CREDIT + kt - 1)
                A(sq[:, kt % 2, :], h[:, kt, :], ACT.Square).then_inc(ss0, 1)
            act.wait_ge(pre_v, 2)
            A(sv[:, 8, :], sv[:, 5, :], ACT.Sin)
            A(sv[:, 9, :], sv[:, 10, :], ACT.Sin).then_inc(pre_e, 1)
            act.preload_act_table_set("natural_log_exp_and_others")
            act.wait_ge(pre_v, 3)
            for ri in range(2):
                for e in range(CH):
                    last = A(pw[:, 1, ri, e, :], pw[:, 0, ri, CH - 1 - e, :], ACT.Copy)
            last.then_inc(pre_e, 1)
            act.wait_ge(n_v, 1)
            root(rsn[:, :], ssum[:, :]).then_inc(n_rs, 1)
            for q in range(NQ):
                for ri in range(2):
                    n = 2 * q + ri
                    if q:
                        act.wait_ge(pre_out[ri], 16 * q)
                    for hf in range(2):
                        act.wait_ge(pre_t, 2 * n + hf + 1)
                        A(bat[:, ri, hf * 4:hf * 4 + 4, :].rearrange("p j c -> p (j c)"), TILE[hf][:, :], ACT.Copy).then_inc(pre_ta, 1)
                    act.wait_ge(pre_ta, 2 * n + 2)
                    act.dma_start(bat_dram[q, :, :, ri, :], bat[:, ri, :, :]).then_inc(pre_out[ri], 16)
                if q:
                    act.wait_ge(pre_kout, 16 * CH * q)
                for n in range(4 * q, 4 * q + 4):
                    act.wait_ge(pre_k, n + 1)
                    g0 = (n // 2 % 2) * 8 + n % 2
                    A(kern[:, g0:g0 + 7:2, :], TILE[2 + n % 2][0:SSM_H, :].rearrange("p (g c) -> p g c", c=P),
                      ACT.Copy).then_inc(pre_ka, 1)
                act.wait_ge(pre_ka, 4 * q + 4)
                act.wait_ge(pre_zero, 16 * 2 * NQ)
                for s_ in range(CH):
                    act.dma_start(toep_dram[q, s_ * SSM_H:(s_ + 1) * SSM_H, :, s_ * SSM_H:],
                                  kern[:, :, 0:(CH - s_) * SSM_H]).then_inc(pre_kout, 16)
            for ri in range(2):
                act.wait_ge(pre_out[ri], 16 * NQ)
            act.wait_ge(pre_kout, 16 * CH * NQ)
            act.wait_ge(pre_cout, 16 * (2 * NQ + 1))
            for g in range(3):
                split_unit_at(g)

            def norm(k, name):
                tok = NORM_TOK.get(name, SEQ)
                if k and name != "b":
                    act.wait_ge(n_v, min(k, 7) + 1)
                    root(rsn[:, 0:tok], ssum[:, 0:tok]).then_inc(n_rs, 1)
                for kt in range(KT):
                    act.wait_ge(n_t, 8 * k + kt + 1)
                    for hf in range(tok // SEQ):
                        cs = slice(hf * SEQ, (hf + 1) * SEQ)
                        b = shift(name, kt, hf)
                        if b is None:
                            last = A(u_hi[:, kt, cs], tmp[:, kt % 2, cs], ACT.Copy)
                        else:
                            last = A(u_hi[:, kt, cs], tmp[:, kt % 2, cs], ACT.Identity, bias=b)
                    last.then_inc(n_hi, 1)

            def attention(units, kbase, swa):
                n_u = len(units)
                for n in range(n_u + 5):
                    if n < n_u:
                        g = n + kbase
                        keys, s_off = units[n][3], units[n][4]
                        act.wait_ge(att_m, g + 1)
                        if g >= 2:
                            act.wait_ge(att_t, g - 1)
                        b = stat[:, g % 4, 0:1]
                        if keys == TOK:
                            A(prob[:, g % 2, 0:SEQ], s_sb[:, g % 2, :], ACT.Exp, bias=b, accum_out=stat[:, g % 4, 1:2])
                            if swa:
                                A(stat[:, g % 4, 6:7], VC("sink", units[n][6][2]), ACT.Exp, bias=b)
                            A(prob[:, g % 2, SEQ:TOK], psum[g % 3][:, SEQ:TOK], ACT.Exp, bias=b,
                              accum_out=stat[:, g % 4, 2:3]).then_inc(att_p, 1)
                        else:
                            A(prob[:, g % 2, 0:SEQ], psum[g % 3][:, SEQ:TOK], ACT.Exp, bias=b,
                              accum_out=stat[:, g % 4, 1:2]).then_inc(att_p, 1)
                    m = n - 1
                    if 0 <= m < n_u:
                        g = m + kbase
                        keys = units[m][3]
                        act.wait_ge(att_t, g + 1)
                        if g >= 2:
                            act.wait_ge(att_o, g - 1)
                        A(prob_t[:, g % 2, 0:keys], psum[3 + g % 2][:, 0:keys], ACT.Copy).then_inc(att_e, 1)
                    m = n - 4
                    if 0 <= m < n_u and m % 2 == 1:
                        pr = (m + kbase) // 2
                        hp, cs = units[m][5]
                        act.wait_ge(att_x, pr + 1)
                        A(u_hi[:, hp, cs], psum[6][:, 0:P], ACT.Copy).then_inc(att_h, 1)

            norm(0, "mix0")
            stage("qk0"); stage("v0")
            attention(ATT0, 0, False)
            stage("wo0"); norm(1, "mlp0")
            stage("up0a"); stage("down0a"); stage("up0b"); stage("down0b")
            norm(2, "mix1")
            stage("q1"); stage("k1"); stage("v1")
            attention(ATT1, 64, True)
            stage("wo1"); norm(3, "mlp1")
            stage("up1a"); stage("down1a"); stage("up1b"); stage("down1b")
            norm(4, "a")
            stage("win")
            stage_end(act, ST["win"], ("a1",))
            act.dma_start(u_dram.rearrange("(k p) s c -> p k s c", p=P), u_sc[:, :, :, :]).then_inc(u_out, 16)
            act.wait_ge(u_out, 16)
            act.wait_ge(S["unit"], value("unit", ST["win"], 8))
            for s_ in range(CH):
                act.dma_start(u_g[s_ * SSM_H:(s_ + 1) * SSM_H, :, :],
                              u_dram[:, s_, :].rearrange("(g h) c -> h g c", h=SSM_H)).then_inc(u_in, 16)
            for q in range(NQ):
                act.wait_ge(ssm_y, q + 1)
                for hf in range(2):
                    last = A(y_g[:, q * 16 + hf:q * 16 + 16:2, :],
                             psum[(2, 6)[q % 2] + hf][:, 0:QJ * NCH].rearrange("p (g c) -> p g c", c=NCH), ACT.Copy)
                last.then_inc(ssm_ya, 1)
                act.wait_ge(ssm_ya, q + 1)
                gs = slice(q * 2 * QJ, (q + 1) * 2 * QJ)
                for t in range(CH):
                    act.dma_start(y_dram[:, t, :].rearrange("(g h) c -> h g c", h=SSM_H)[:, gs, :],
                                  y_g[t * SSM_H:(t + 1) * SSM_H, gs, :]).then_inc(y_out, 16)
            act.wait_ge(y_out, 16 * CH * NQ)
            act.dma_start(y2[:, :, :, :], y_dram.rearrange("(k p) s c -> p k s c", p=P)).then_inc(y_in, 16)
            for k in range(KT + 1):
                if k < KT:
                    e, y = ge_flat(3, k), rs[:, k % 2, 0:SEQ]
                    act.wait_ge(ge2, k + 1)
                    chain.link(A(e, ge_flat(2, k), ACT.Exp, scale=-2.0 * 0.7978845608028654))
                    chain.link(A(y, e, ACT.Ln, bias=C("ones")[:, 0:1]))
                    A(y, y, ACT.Exp, scale=-1.0).then_inc(ge3, 1)
                t = k - 1
                if t >= 0:
                    act.wait_ge(ge4, t + 1)
                    A(u_hi[:, t, 0:SEQ].rearrange("p (c s) -> p s c", s=CH), ge[:, 4, t % 2, :, :], ACT.Copy).then_inc(ge5, 1)
            stage("glu")
            for kt in range(KT):
                act.wait_ge(S["d1"], value("d1", ST["glu"], kt + 1))
                act.wait_ge(S["sq"], value("sq", ST["glu"], kt - 1))
                A(sq[:, kt % 2, 0:SEQ], h[:, kt, 0:SEQ], ACT.Square).then_inc(S["a3"], 1)
            norm(5, "ffn0")
            stage("fup0"); stage("fdown0"); norm(6, "kv")
            stage("k2"); stage("v2"); norm(7, "b"); stage("q2")
            for n in range(HEADS + 2):
                if n < HEADS:
                    act.wait_ge(sb_d1, n + 1)
                    chain.link(A(sb_e[:, n % 2, :], sb_n[:, n % 2, :], ACT.Exp))
                    A(sb_e[:, n % 2, :], sb_e[:, n % 2, :], ACT.Ln, bias=C("ones")[:, 0:1]).then_inc(sb_a1, 1)
                m = n - 1
                if 0 <= m < HEADS:
                    act.wait_ge(sb_d3, m + 1)
                    if m >= 2:
                        act.wait_ge(sb_o, m - 1)
                    A(sb_w[:, m % 2, :], sb_n[:, m % 2, :], ACT.Exp).then_inc(sb_a2, 1)
                m = n - 2
                if 0 <= m and m % 2 == 1:
                    pr = m // 2
                    act.wait_ge(sb_o, m + 1)
                    A(u_hi[:, pr, 0:SEQ], psum[4 + pr % 2][:, 0:SEQ], ACT.Copy).then_inc(sb_h, 1)
            stage("wo2"); norm(8, "ffn1")
            stage("fup1"); stage("fdown1")

        @block.vector
        def _(dve):
            for n in ("lo", "mod", "d1", "d2", "d3"):
                dve.nop().then_inc(S[n], CREDIT)
            chain = Chain(dve, dve_chain)
            link = chain.link
            TT, STT, TS = dve.tensor_tensor, dve.scalar_tensor_tensor, dve.tensor_scalar
            dve.memset(half_eps[:, :], -0.5 * EPS).then_inc(const_set, 1)

            def lower(g_static, i, per):
                slot = g_static % RING
                dve.wait_ge(S["hi"], i * per + (CREDIT + g_static + 1))
                TT(w_lo[:, slot, :], raw[:, slot, :], w_hi[:, slot, :].bitcast(F32), ALU.subtract).then_inc(S["lo"], 1)

            def mods(layer, m, turn):
                dve.wait_ge(S["ada"], turn)
                TT(mod[:, layer, bass.ds(m, 4), :], ADA_BANK[:, 0:8].rearrange("p (m c) -> p m c", c=2),
                   adab[:, layer, bass.ds(m, 4), :], ALU.add).then_inc(S["mod"], 1)

            def dcol(t, j, cols):
                return t[:, bass.ds(j, 1), cols].rearrange("p a t -> p (a t)")

            def tile(s, i, jj, body, first=False):
                j = i * body + jj
                bank = TILE[(s.tile0 + jj) % RING]
                b2 = (s.tile0 + jj) % 2
                n_done = i * (body * s.units) + (CREDIT + s.unit0 + (jj + 1) * s.units)
                all_ = slice(0, s.tok)
                if s.kind == "QK":
                    dve.wait_ge(S["a1"], value("a1", s, j + 1))
                    dve.tensor_copy(dcol(QK_DST[s.name], j, all_), bank[:, all_]).then_inc(S["d1"], 1)
                    if jj:
                        qk_scale(s, i, jj - 1, body)
                elif s.kind == "RES":
                    dve.wait_ge(S["unit"], n_done)
                    gate = s.more.get("gate")
                    if gate is None:
                        TT(dcol(h, j, all_), bank[:, all_], dcol(h, j, all_), ALU.add).then_inc(S["d1"], 1)
                    else:
                        for hf in range(s.tok // SEQ):
                            cs = slice(hf * SEQ, (hf + 1) * SEQ)
                            last = STT(dcol(h, j, cs), bank[:, cs], mod[:, gate[0], bass.ds(j + gate[1] * 8, 1), hf],
                                       dcol(h, j, cs), ALU.mult, ALU.add)
                        last.then_inc(S["d1"], 1)
                elif s.kind == "MLP":
                    dve.wait_ge(S["a1"], value("a1", s, j + 1))
                    dve.wait_ge(S["d1"], value("d1", s, j - 1))
                    link(TT(tmp[:, b2, all_], rs[:, b2, all_], rs[:, b2, all_], ALU.mult))
                    TT(dcol(hid_lo, j, all_), tmp[:, b2, all_], dcol(hid_hi, j, all_).bitcast(F32), ALU.subtract).then_inc(S["d1"], 1)
                elif s.kind == "UP":
                    if jj == 1:
                        if not first:
                            gated(s, i * 2 - 1, 1)
                        gate_conv(s, i, 0)
                    if jj == 3:
                        gate_conv(s, i, 1)
                        gated(s, i * 2, 0)
                elif s.kind == "GLU" and jj % 2:
                    pb = (jj // 2) % 2
                    dve.wait_ge(S["unit"], n_done)
                    TS(tmp[:, pb, 0:SEQ], bank[:, 0:SEQ], LOW, None, ALU.max).then_inc(S["d2"], 1)
                    if jj == 3:
                        glu_out(s, i, 0)
                        glu_out(s, i, 1)

            def gate_conv(s, i, pb):
                layer, pair = int(s.name[-1]), i * 2 + pb
                dve.wait_ge(S["a1"], value("a1", s, i * 4 + 2 * (pb + 1)))
                link(TS(f_c[:, pb, :], f_gate[:, pb, 2:2 + SEQ], VC("conv_w", (layer * 3 + 2) * FT + pair),
                        VC("conv_b", layer * FT + pair), ALU.mult, ALU.add))
                link(STT(f_c[:, pb, :], f_gate[:, pb, 1:1 + SEQ], VC("conv_w", (layer * 3 + 1) * FT + pair), f_c[:, pb, :],
                         ALU.mult, ALU.add))
                link(STT(f_c[:, pb, :], f_gate[:, pb, 0:SEQ], VC("conv_w", (layer * 3) * FT + pair), f_c[:, pb, :],
                         ALU.mult, ALU.add))
                TS(f_e[:, pb, :], f_c[:, pb, :], LOW, None, ALU.max).then_inc(S["d1"], 1)

            def gated(s, pair, pb):
                dve.wait_ge(S["g1"], value("g1", s, pair + 1))
                link(TT(f_h[:, pb, :], f_h[:, pb, :], f_y[:, pb, :], ALU.mult))
                TT(f_h[:, pb, :], f_h[:, pb, :], f_t[:, pb, :], ALU.mult).then_inc(S["d2"], 1)

            def glu_out(s, i, pb):
                pair = i * 2 + pb
                v = rs[:, pb, 0:SEQ]
                dve.wait_ge(S["a1"], value("a1", s, i * 2 + (pb + 1)))
                dve.wait_ge(S["g1"], value("g1", s, i * 2 + (pb + 1)))
                link(TT(v, v, f_y[:, pb, :], ALU.mult))
                link(TT(v, v, f_t[:, pb, :], ALU.mult))
                TT(dcol(h, pair, slice(0, SEQ)), v, dcol(h, pair, slice(0, SEQ)), ALU.add).then_inc(S["d1"], 1)

            def qk_scale(s, i, jj, body):
                j = i * body + jj
                b2 = (s.tile0 + jj) % 2
                dst = dcol(QK_DST[s.name], j, slice(0, s.tok))
                dve.wait_ge(S["a2"], value("a2", s, j + 1))
                dve.wait_ge(S["d1"], value("d1", s, j + 1))
                v, y, y2_ = tmp[:, b2, 0:s.tok], rs[:, b2, 0:s.tok], sq[:, b2, 0:s.tok]
                link(TT(v, v, y2_, ALU.mult))
                link(STT(dst, dst, VC(QK_GAIN[s.name][0], j + QK_GAIN[s.name][1]), y, ALU.mult, ALU.mult))
                STT(dst, v, 1.5, dst, ALU.add, ALU.mult).then_inc(S["d2"], 1)

            LINKS = {"QK": 8, "MLP": 4, "UP": 8, "GLU": 4}

            def stage(name):
                s = ST[name]
                body = min(4, s.tiles)
                per = body * s.units
                if row_sums(s):
                    link(dve.memset(ssum[:, :], 0.0))
                if s.more.get("gate"):
                    dve.wait_ge(S["mod"], CREDIT + 12 * s.more["gate"][0] + 2 * (s.more["gate"][1] + 1))
                if s.kind == "UP":
                    link(dve.memset(f_gate[:, :, 0:2], 0.0))
                n_links = LINKS.get(s.kind, 0) + (1 if row_sums(s) else 0)

                def one(i, first=False, last=False):
                    for jj in range(body):
                        for k in range(s.units):
                            n = jj * s.units + k
                            if not last:
                                lower(s.unit0 + n + 3, i, per)
                            elif s.unit0 + per + n + 3 < n_units:
                                lower(s.unit0 + per + n + 3, 0, 0)
                        tile(s, i, jj, body, first)
                    if s.ada is not None:
                        mods(s.ada[0], i * 4 + s.ada[1], i * 4 + (CREDIT + s.base["ada"] + 4))
                    if s.kind == "QK":
                        qk_scale(s, i, body - 1, body)
                    if row_sums(s):
                        dve.wait_ge(S["sq"], value("sq", s, i * 4 + 4))
                        link(TT(ssum[:, 0:s.tok], SS[:, 0:s.tok], ssum[:, 0:s.tok], ALU.add))
                        dve.nop().then_inc(S["d3"], 1)

                if name == "fdown1":
                    one(0)
                    one(1, last=True)
                elif s.kind == "UP":
                    one(0, first=True)
                    with repeat(dve, s.tiles // body - 1, chain, n_links) as i:
                        one(i + 1)
                    gated(s, s.tiles // 2 - 1, 1)
                else:
                    with repeat(dve, s.tiles // body, chain, n_links) as i:
                        one(i)

            def gains(layer, which):
                g = ("g_mix", "g_mlp")[which]
                a = VEC[g][0] + layer * 16
                sc = mod[:, layer, 8 + 24 * which:16 + 24 * which, :].rearrange("p k c -> p (k c)")
                STT(gain[:, layer, which, :, :].rearrange("p k c -> p (k c)"), sc, 1.0, vec[:, a:a + 16],
                    ALU.add, ALU.mult).then_inc(gain_done, 1)

            def newton(k, tok):
                v, y = ssum[:, 0:tok], rsn[:, 0:tok]
                dve.wait_ge(n_rs, min(k, 7) + 1)
                link(TT(v, v, y, ALU.mult))
                link(TT(v, v, y, ALU.mult))
                link(STT(y, v, 1.5, y, ALU.add, ALU.mult))

            def norm(k, name):
                tok = NORM_TOK.get(name, SEQ)
                if mod_norm(name):
                    layer, which = mod_norm(name)
                    dve.wait_ge(S["mod"], CREDIT + MODS_NEEDED[name])
                    gains(layer, which)
                    dve.wait_ge(gain_done, k + 1)
                if k and name != "b":
                    v = ssum[:, 0:tok]
                    if name == "ffn0":
                        dve.wait_ge(S["sq"], value("sq", ST["glu"], KT))
                    TS(v, SS[:, 0:tok] if name == "ffn0" else v, -0.5 * INV_D, -0.5 * EPS, ALU.mult, ALU.add).then_inc(n_v, 1)
                    newton(k, tok)
                if name == "b":
                    dve.wait_ge(S["unit"], value("unit", ST["v2"], 8))
                for kt in range(KT + 1):
                    if kt < KT:
                        if kt >= 2 or k:
                            dve.wait_ge(n_hi, 8 * k + kt - 1)
                            dve.wait_ge(n_lo, 8 * k + kt - 1)
                        for hf in range(tok // SEQ):
                            cs = slice(hf * SEQ, (hf + 1) * SEQ)
                            last = STT(tmp[:, kt % 2, cs], h[:, kt, cs], norm_gain(name, kt, hf), rsn[:, cs], ALU.mult, ALU.mult)
                        last.then_inc(n_t, 1)
                    t = kt - 1
                    if t >= 0:
                        dve.wait_ge(n_hi, 8 * k + t + 1)
                        for hf in range(tok // SEQ):
                            cs = slice(hf * SEQ, (hf + 1) * SEQ)
                            b = shift(name, t, hf)
                            hi = u_hi[:, t, cs].bitcast(F32)
                            if b is None:
                                last = TT(u_lo[:, t, cs], tmp[:, t % 2, cs], hi, ALU.subtract)
                            else:
                                last = STT(u_lo[:, t, cs], tmp[:, t % 2, cs], b, hi, ALU.add, ALU.subtract)
                        last.then_inc(n_lo, 1)

            dve.wait_ge(small_in, 48)
            for name, a, n in (("gqk0", 0, 8), ("gqk1", 0, 8), ("gqk2", 8, 8)):
                c0 = VEC[name][0] + a
                link(TS(vec[:, c0:c0 + n], vec[:, c0:c0 + n], HD ** -0.5, None, ALU.mult))
            sl = silu[:, :, :].rearrange("p k c -> p (k c)")
            a0 = VEC["c"][0]
            TS(sl, vec[:, a0:a0 + 16], LOW, None, ALU.max).then_inc(const_set, 1)
            dve.wait_ge(silu_e, 1)
            link(TS(sl, sl, 1.0, None, ALU.add))
            link(dve.reciprocal(sl, sl))
            TT(sl, sl, vec[:, a0:a0 + 16], ALU.mult).then_inc(silu_d, 1)

            dve.wait_ge(pre_e, 1)
            v = lambda n: sv[:, n, :]
            link(TT(v(4), v(0), v(3), ALU.mult))
            dve.nop().then_inc(pre_v, 1)
            link(TT(v(11), v(1), v(3), ALU.mult))
            ROUND = 12582912.0
            link(TS(v(12), v(11), 1.0 / (2 * np.pi), None, ALU.mult))
            link(TS(v(12), v(12), ROUND, None, ALU.add))
            link(TS(v(12), v(12), ROUND, None, ALU.subtract))
            two_pi = 2 * np.pi
            p1 = float(np.float32(np.round(two_pi * 512) / 512))
            p2 = float(np.float32(np.round((two_pi - p1) * 2 ** 21) / 2 ** 21))
            p3 = float(np.float32(two_pi - p1 - p2))
            for part in (p1, p2, p3):
                link(STT(v(11), v(12), -part, v(11), ALU.mult, ALU.add))
            PI = 3.1415925
            link(TS(v(5), v(11), PI, -PI, ALU.min, ALU.max))
            link(STT(v(13), v(5), -1.0, v(5), ALU.mult, ALU.max))
            link(TS(v(10), v(13), -1.0, float(np.pi / 2), ALU.mult, ALU.add))
            dve.nop().then_inc(pre_v, 1)
            dve.wait_ge(pre_e, 3)

            def cmul(dr, di, ar, ai, br, bi, t):
                link(TT(dr, ar, br, ALU.mult))
                link(TT(t, ai, bi, ALU.mult))
                link(TT(dr, dr, t, ALU.subtract))
                link(TT(di, ar, bi, ALU.mult))
                link(TT(t, ai, br, ALU.mult))
                link(TT(di, di, t, ALU.add))

            pr_, pi_ = pw[:, 0, 0, :, :], pw[:, 0, 1, :, :]
            link(dve.memset(pr_[:, 0, :], 1.0))
            link(dve.memset(pi_[:, 0, :], 0.0))
            link(TT(pr_[:, 1, :], v(6), v(9), ALU.mult))
            link(TT(pi_[:, 1, :], v(6), v(8), ALU.mult))
            n = 1
            while n < CH:
                b = [p_[:, n, :].unsqueeze(1).to_broadcast([P, n, PAIRS]) for p_ in (pr_, pi_)]
                cmul(pr_[:, n + 1:2 * n + 1, :], pi_[:, n + 1:2 * n + 1, :], pr_[:, 1:n + 1, :], pi_[:, 1:n + 1, :],
                     b[0], b[1], pw[:, 2, 0, 1:n + 1, :])
                n *= 2
            dve.nop().then_inc(pre_v, 1)
            dve.wait_ge(S["sq"], CREDIT + KT)
            TS(ssum[:, :], SS[:, :], -0.5 * INV_D, -0.5 * EPS, ALU.mult, ALU.add).then_inc(n_v, 1)
            link(TS(v(14), pr_[:, 1, :], -1.0, None, ALU.add))
            link(TT(v(15), v(0), v(0), ALU.mult))
            link(TT(v(16), v(1), v(1), ALU.mult))
            link(TT(v(15), v(15), v(16), ALU.add))
            link(dve.reciprocal(v(15), v(15)))
            link(TS(v(16), v(1), -1.0, None, ALU.mult))
            cmul(v(17), v(18), v(14), pi_[:, 1, :], v(0), v(16), v(19))
            link(TT(v(17), v(17), v(15), ALU.mult))
            link(TT(v(18), v(18), v(15), ALU.mult))
            dve.wait_ge(ssm_par_in, 32)
            bshape = [P, PAIRS, SSM_H]
            cmul(bbar[:, 0], bbar[:, 1], bc[:, 0], bc[:, 1], v(17).unsqueeze(2).to_broadcast(bshape),
                 v(18).unsqueeze(2).to_broadcast(bshape), ktmp[:, 0:4, :, :].rearrange("p a s h -> p (a s) h"))
            dve.nop().then_inc(pre_v, 1)
            for q in range(NQ):
                js = slice(q * QJ, (q + 1) * QJ)
                shp = [P, QJ, POW, SSM_H]
                cr, ci = (bc[:, k, js, :].unsqueeze(2).to_broadcast(shp) for k in (2, 3))
                ar, ai = (pw[:, 0, k, :, js].rearrange("p e j -> p j e").unsqueeze(3).to_broadcast(shp) for k in (0, 1))
                dr, di, t = ca[:, js, 0], ca[:, js, 1], ctmp[:, :, :, :]
                link(TT(dr, cr, ar, ALU.mult))
                link(TT(t, ci, ai, ALU.mult))
                link(TT(dr, dr, t, ALU.subtract))
                link(TT(di, cr, ai, ALU.mult))
                link(TT(t, ci, ar, ALU.mult))
                link(STT(di, di, -1.0, t, ALU.mult, ALU.subtract))
                dve.nop().then_inc(pre_c, 1)
            cmul(v(20), v(21), v(9), v(8), v(9), v(8), v(22))
            cmul(v(17), v(18), v(20), v(21), v(20), v(21), v(22))
            cmul(rot0[:, 0, :, 0], rot0[:, 1, :, 0], v(17), v(18), v(17), v(18), v(22))
            n = 1
            while n < NCH:
                b = [rot0[:, k, :, n - 1].unsqueeze(2).to_broadcast([P, PAIRS, n]) for k in (0, 1)]
                cmul(rot0[:, 0, :, n:2 * n], rot0[:, 1, :, n:2 * n], rot0[:, 0, :, 0:n], rot0[:, 1, :, 0:n], b[0], b[1],
                     rot0[:, 2, :, 0:n])
                n *= 2
            link(dve.tensor_copy(rot0[:, 2, :, :], v(7).unsqueeze(2).to_broadcast([P, PAIRS, NCH])))
            link(dve.memset(rot0[:, 2, :, 0:1], 0.0))
            dve.nop().then_inc(pre_v, 1)
            newton(0, TOK)
            dve.wait_ge(S["ada"], CREDIT + 16)
            TT(mod[:, 0, 0:16, :], ADA_BANK[:, 0:32].rearrange("p (m c) -> p m c", c=2), adab[:, 0, 0:16, :],
               ALU.add).then_inc(S["mod"], 4)
            for ri in range(2):
                dve.wait_ge(pre_out[ri], 16 * NQ)
            dve.wait_ge(pre_kout, 16 * CH * NQ)
            dve.wait_ge(pre_cout, 16 * (2 * NQ + 1))
            for g in range(3):
                lower(g, 0, 0)

            def attention(units, kbase, swa):
                n_u = len(units)
                for n in range(n_u + 5):
                    if n < n_u:
                        g = n + kbase
                        keys, s_off, kind = units[n][3], units[n][4], units[n][6]
                        st = stat[:, g % 4, :]
                        dve.wait_ge(att_s, g + 1)
                        if g >= 2:
                            dve.wait_ge(att_p, g - 1)
                        if kind[0] != "ctx":
                            if kind[0] == "na":
                                b = kind[1]
                                dve.wait_ge(bias_in[b % 3], 16 * (b // 3 + 1))
                                b_ap = bias_sb[:, b % 3, :]
                            else:
                                b_ap = C("window")[:, kind[1] * 256:kind[1] * 256 + 256]
                            TT(s_sb[:, g % 2, :], psum[g % 3][:, 0:SEQ], b_ap, ALU.add)
                            link(dve.tensor_reduce(st[:, 4:5], psum[g % 3][:, SEQ:TOK], AX.X, ALU.max))
                            link(dve.tensor_reduce(st[:, 3:4], s_sb[:, g % 2, :], AX.X, ALU.max))
                            if kind[0] == "swa":
                                link(TT(st[:, 4:5], st[:, 4:5], VC("sink", kind[2]), ALU.max))
                            TS(st[:, 0:1], st[:, 3:4], st[:, 4:5], -1.0, ALU.max, ALU.mult).then_inc(att_m, 1)
                        else:
                            link(dve.tensor_reduce(st[:, 3:4], psum[g % 3][:, SEQ:TOK], AX.X, ALU.max))
                            TS(st[:, 0:1], st[:, 3:4], -1.0, None, ALU.mult).then_inc(att_m, 1)
                    m = n - 2
                    if 0 <= m < n_u:
                        g = m + kbase
                        st = stat[:, g % 4, :]
                        kind = units[m][6]
                        keys = units[m][3]
                        pr = g // 2
                        dve.wait_ge(att_p, g + 1)
                        if keys == TOK:
                            link(TT(st[:, 1:2], st[:, 1:2], st[:, 2:3], ALU.add))
                        if kind[0] == "swa":
                            link(TT(st[:, 1:2], st[:, 1:2], st[:, 6:7], ALU.add))
                        link(dve.reciprocal(st[:, 7:8], st[:, 1:2]))
                        dve.wait_ge(att_o, g + 1)
                        if pr >= 2 and g % 2 == 0:
                            dve.wait_ge(att_x, pr - 1)
                        TS(o_pair[:, pr % 2, (g % 2) * HD:(g % 2 + 1) * HD], (psum[5], psum[7])[g % 2][:, (g % 2) * HD:(g % 2 + 1) * HD], st[:, 7:8], None,
                           ALU.mult).then_inc(att_n, 1)
                    m = n - 4
                    if 0 <= m < n_u and m % 2 == 1:
                        pr = (m + kbase) // 2
                        hp, cs = units[m][5]
                        dve.wait_ge(att_h, pr + 1)
                        TT(u_lo[:, hp, cs], psum[6][:, 0:P], u_hi[:, hp, cs].bitcast(F32), ALU.subtract).then_inc(att_l, 1)

            norm(0, "mix0")
            stage("qk0"); stage("v0")
            attention(ATT0, 0, False)
            stage("wo0"); norm(1, "mlp0")
            stage("up0a"); stage("down0a"); stage("up0b"); stage("down0b")
            norm(2, "mix1")
            stage("q1"); stage("k1"); stage("v1")
            dve.wait_ge(S["d2"], value("d2", ST["k1"], 2))
            for m in range(10):
                dst = q1[:, m, :] if m < 8 else k1[:, m - 8, 0:SEQ]
                dve.wait_ge(rope_p, m + 1)
                link(TT(tmp[:, m % 2, 0:SEQ], (SS, SS2)[m % 2][:, 0:SEQ], C("sin"), ALU.mult))
                link(TT(dst, dst, C("cos"), ALU.mult))
                TT(dst, dst, tmp[:, m % 2, 0:SEQ], ALU.add).then_inc(rope_d, 1)
            attention(ATT1, 64, True)
            stage("wo1"); norm(3, "mlp1")
            stage("up1a"); stage("down1a"); stage("up1b"); stage("down1b")
            norm(4, "a")
            stage("win")

            dve.wait_ge(rot_in, 16)
            dve.wait_ge(u_in, 16 * CH)
            link(dve.memset(h_st[:, :, :, :, 0:1].rearrange("p a b j c -> p (a b) j c"), 0.0))
            for q in range(NQ):
                b = q % 2
                js = slice(q * QJ, (q + 1) * QJ)
                vr, vi, rr = (rot[:, k, js, :] for k in range(3))
                xs = psum[b][:, :].rearrange("p (j r c) -> p r j c", j=QJ, r=2)
                flat = lambda a: a.rearrange("p j c -> p (j c)")
                dve.wait_ge(ssm_x, q + 1)
                xr, xi = x_mod[:, b, 0], x_mod[:, b, 1]
                TT(xr, xs[:, 0], vr, ALU.mult)
                link(TT(x_tmp[:, 0], xs[:, 1], vi, ALU.mult))
                link(TT(xr, xr, x_tmp[:, 0], ALU.add))
                TT(xi, xs[:, 1], vr, ALU.mult)
                link(TT(x_tmp[:, 1], xs[:, 0], vi, ALU.mult))
                link(TT(xi, xi, x_tmp[:, 1], ALU.subtract))
                gr, gi = g_st[:, b, 0], g_st[:, b, 1]
                dve.tensor_tensor_scan(flat(gr), flat(rr), flat(xr), 0.0, ALU.mult, ALU.add)
                link(dve.tensor_tensor_scan(flat(gi), flat(rr), flat(xi), 0.0, ALU.mult, ALU.add))
                if q >= 2:
                    dve.wait_ge(ssm_y, q - 1)
                fr, to = slice(0, NCH - 1), slice(1, NCH)
                hr, hi = h_st[:, b, 0, :, to], h_st[:, b, 1, :, to]
                TT(hr, gr[:, :, fr], vr[:, :, fr], ALU.mult)
                link(TT(g_tmp[:, 0, :, fr], gi[:, :, fr], vi[:, :, fr], ALU.mult))
                link(TT(hr, hr, g_tmp[:, 0, :, fr], ALU.subtract))
                TT(hi, gr[:, :, fr], vi[:, :, fr], ALU.mult)
                link(TT(g_tmp[:, 1, :, fr], gi[:, :, fr], vr[:, :, fr], ALU.mult))
                TT(hi, hi, g_tmp[:, 1, :, fr], ALU.add).then_inc(ssm_h, 1)
            dve.wait_ge(y_in, 16)
            for k in range(KT + 1):
                if k < KT:
                    b = k % 2
                    y_, t_, z_ = (ge[:, n, b, :, :] for n in range(3))
                    link(STT(y_, u_sc[:, k], VC("a_d", k), y2[:, k], ALU.mult, ALU.add))
                    link(TT(t_, y_, y_, ALU.mult))
                    link(TS(t_, t_, 0.044715, 1.0, ALU.mult, ALU.add))
                    link(TT(z_, t_, y_, ALU.mult))
                    TS(z_, z_, LOW / 1.6, None, ALU.max).then_inc(ge2, 1)
                t = k - 1
                if t >= 0:
                    dve.wait_ge(ge_n, t + 1)
                    if t >= 2:
                        dve.wait_ge(ge6, t - 1)
                    g_ = ge_flat(4, t)
                    link(TT(g_, ge_flat(0, t), rs[:, t % 2, 0:SEQ], ALU.mult))
                    TT(g_, g_, rs[:, t % 2, SEQ:TOK], ALU.mult).then_inc(ge4, 1)
            stage("glu"); norm(5, "ffn0")
            stage("fup0"); stage("fdown0"); norm(6, "kv")
            stage("k2"); stage("v2"); norm(7, "b"); stage("q2")

            for n in range(HEADS + 2):
                if n < HEADS:
                    b = n % 2
                    dve.wait_ge(sb_s, n + 1)
                    if n >= 2:
                        dve.wait_ge(sb_c, n - 1)
                        dve.wait_ge(sb_a2, n - 1)
                    link(TS(sb_r[:, b, :], psum[n % 3][:, 0:384], 0.0, None, ALU.max))
                    STT(sb_n[:, b, :], sb_r[:, b, :], -2.0, psum[n % 3][:, 0:384], ALU.mult, ALU.add).then_inc(sb_d1, 1)
                m = n - 1
                if 0 <= m < HEADS:
                    dve.wait_ge(sb_c, m + 1)
                    TT(sb_n[:, m % 2, :], psum[m % 3][:, 0:384], C("causal_neg"), ALU.add).then_inc(sb_d3, 1)
                if n < HEADS:
                    dve.wait_ge(sb_a1, n + 1)
                    link(TT(sb_r[:, b, :], sb_r[:, b, :], sb_e[:, b, :], ALU.add))
                    TT(sb_r[:, b, :], sb_r[:, b, :], C("causal"), ALU.mult).then_inc(sb_d2, 1)
                m = n - 2
                if 0 <= m and m % 2 == 1:
                    pr = m // 2
                    dve.wait_ge(sb_h, pr + 1)
                    TT(u_lo[:, pr, 0:SEQ], psum[4 + pr % 2][:, 0:SEQ], u_hi[:, pr, 0:SEQ].bitcast(F32), ALU.subtract).then_inc(sb_l, 1)
            stage("wo2"); norm(8, "ffn1")
            stage("fup1"); stage("fdown1")

        @block.gpsimd
        def _(pool):
            pool.dma_start(sv[:, 0:3, :], ssm_in).then_inc(ssm_par_in, 16)
            pool.dma_start(bc[:, :, :, :], ssm_bc).then_inc(ssm_par_in, 16)
            pool.nop().then_inc(S["g1"], CREDIT)
            pool.nop().then_inc(S["g2"], CREDIT)
            chain = Chain(pool, pool_chain)
            link = chain.link

            def newton(s, i, pb):
                e = f_e[:, pb, :] if s.kind == "UP" else tmp[:, pb, 0:SEQ]
                y, t = f_y[:, pb, :], f_t[:, pb, :]
                pool.wait_ge(S["a2"], value("a2", s, i * 2 + (pb + 1)))
                link(pool.tensor_tensor(t, e, y, ALU.mult))
                link(pool.tensor_tensor(t, t, y, ALU.add))
                pool.tensor_tensor(t, two[:, 0:1].to_broadcast([P, SEQ]), t, ALU.subtract).then_inc(S["g1"], 1)

            def gate_value(s, i, pb):
                pool.wait_ge(S["d1"], value("d1", s, i * 2 + (pb + 1)))
                pool.wait_ge(S["g2"], value("g2", s, i * 2 + (pb - 1)))
                link(pool.tensor_tensor(f_h[:, pb, :], f_c[:, pb, :], f_val[:, pb, :], ALU.mult))

            def hidden_lo(s, pair, pb):
                pool.wait_ge(S["a3"], value("a3", s, pair + 1))
                at = bass.ds(pair, 1)
                pool.tensor_tensor(f_lo[:, at, :].rearrange("p a t -> p (a t)"), f_h[:, pb, :],
                                   f_hi[:, at, :].rearrange("p a t -> p (a t)").bitcast(F32), ALU.subtract).then_inc(S["g2"], 1)

            def glu_stage(s):
                with repeat(pool, s.tiles // 4, chain, 4) as i:
                    newton(s, i, 0)
                    newton(s, i, 1)

            def up_stage(s):
                def one(i, first=False):
                    if not first:
                        hidden_lo(s, i * 2 - 2, 0)
                        hidden_lo(s, i * 2 - 1, 1)
                    gate_value(s, i, 0)
                    newton(s, i, 0)
                    gate_value(s, i, 1)
                    newton(s, i, 1)

                one(0, first=True)
                with repeat(pool, s.tiles // 4 - 1, chain, 6) as i:
                    one(i + 1)
                hidden_lo(s, s.tiles // 2 - 2, 0)
                hidden_lo(s, s.tiles // 2 - 1, 1)

            link(pool.memset(two[:, :], 2.0))
            zeros = rs[:, :, :].rearrange("p a t -> p (a t)")
            link(pool.memset(zeros, 0.0))
            for q in range(NQ):
                for k in range(2):
                    pool.dma_start(toep_dram[q, :, k * QJ:(k + 1) * QJ, :].rearrange("p g c -> p (g c)"), zeros).then_inc(pre_zero, 16)
            pool.wait_ge(pre_e, 4)
            pool.wait_ge(pre_v, 4)
            TT = pool.tensor_tensor
            for q in range(NQ):
                js = slice(q * QJ, (q + 1) * QJ)
                shp = [P, QJ, CH, SSM_H]
                br, bi = (bbar[:, k, js, :].unsqueeze(2).to_broadcast(shp) for k in (0, 1))
                ar, ai = (pw[:, 1, k, 0:CH, js].rearrange("p e j -> p j e").unsqueeze(3).to_broadcast(shp) for k in (0, 1))
                dr, di, t = ba[:, js, 0], ba[:, js, 1], ktmp[:, :, :, :]
                link(TT(dr, br, ar, ALU.mult))
                link(TT(t, bi, ai, ALU.mult))
                link(TT(dr, dr, t, ALU.subtract))
                link(TT(di, br, ai, ALU.mult))
                link(TT(t, bi, ar, ALU.mult))
                TT(di, di, t, ALU.add).then_inc(pre_b, 1)
            for q in range(NQ):
                pool.wait_ge(pre_c, q + 1)
                for ri in range(2):
                    pool.dma_start(ca_dram[q, :, :, ri, :], ca[:, q * QJ:(q + 1) * QJ, ri, 1:POW, :].rearrange("p j e h -> p j (e h)")).then_inc(pre_cout, 16)
            pool.wait_ge(pre_v, 5)
            pool.dma_start(rot_dram, rot0[:, :, :, :]).then_inc(pre_cout, 16)
            for b in range(2 * HEADS):
                if b == 0:
                    stage_end(pool, ST["v0"], ("a1",))
                if b >= 3:
                    pool.wait_ge(att_m, b - 2)
                pool.dma_start(bias_sb[:, b % 3, :], bias_na[b]).then_inc(bias_in[b % 3], 16)
            stage_end(pool, ST["down0b"], ("ada",))
            pool.dma_start(rot[:, :, :, :], rot_dram).then_inc(rot_in, 16)
            stage_end(pool, ST["down1b"], ("unit",))
            def load_tables(q, tables, landed):
                for dst, src in tables:
                    letters = "p j r c" if len(dst.shape) == 5 else "p j c"
                    pool.dma_start(dst[:, q % 2].rearrange(f"{letters} -> p ({letters[2:]})"),
                                   src[q].rearrange(f"{letters} -> p ({letters[2:]})")).then_inc(landed[q % 2], 16)

            outputs = ((s_ca, ca_dram), (s_toep, toep_dram))
            for q in range(NQ + 1):
                if q < NQ:
                    if q >= 2:
                        pool.wait_ge(ssm_x, q - 1)
                    load_tables(q, ((s_bat, bat_dram),), bat_in)
                if q >= 1:
                    if q >= 3:
                        pool.wait_ge(ssm_y, q - 2)
                    load_tables(q - 1, outputs, ssm_in_s)
            for k in range(KT + 1):
                if k < KT:
                    y, t = rs[:, k % 2, 0:SEQ], rs[:, k % 2, SEQ:TOK]
                    pool.wait_ge(ge3, k + 1)
                    link(pool.tensor_tensor(t, ge_flat(3, k), y, ALU.mult))
                    link(pool.tensor_tensor(t, t, y, ALU.add))
                    pool.tensor_tensor(t, two[:, 0:1].to_broadcast([P, SEQ]), t, ALU.subtract).then_inc(ge_n, 1)
                m = k - 1
                if m >= 0:
                    pool.wait_ge(ge5, m + 1)
                    pool.tensor_tensor(u_lo[:, m, 0:SEQ].rearrange("p (c s) -> p s c", s=CH), ge[:, 4, m % 2, :, :],
                                       u_hi[:, m, 0:SEQ].bitcast(F32).rearrange("p (c s) -> p s c", s=CH),
                                       ALU.subtract).then_inc(ge6, 1)
            glu_stage(ST["glu"])
            up_stage(ST["fup0"])
            up_stage(ST["fup1"])


def pack_units(w, k_tiles):
    k, n = w.shape
    w = w.reshape(k // P, P, n // P, P)
    pad = (-(k // P)) % k_tiles
    w = np.pad(w, ((0, pad), (0, 0), (0, 0), (0, 0)))
    w = w.reshape(-1, k_tiles, P, n // P, P).transpose(3, 0, 2, 1, 4)
    return w.reshape(-1, P, k_tiles * P)


def pack_value_units(w):
    w = w.reshape(2, KT // 2, P, w.shape[1] // VW, VW).transpose(3, 0, 2, 1, 4)
    return w.reshape(-1, P, KT // 2 * VW)


def interleave(a, b):
    k = a.shape[0]
    return np.stack([a.reshape(k, -1, P), b.reshape(k, -1, P)], axis=2).reshape(k, -1)


def columns(v):
    return np.ascontiguousarray(v.reshape(-1, P).T)


SWA_ORDER = [x for lo in (0, 8) for k in range(4) for x in (lo + k, lo + 4 + k)]


def shape_constants():
    i = np.arange(P)
    out = np.zeros((P, N_CON), np.float32)

    def put(name, a):
        at, n = CON[name]
        out[:, at:at + n] = a

    put("ident", np.eye(P))
    put("ones", np.ones((P, P)))
    put("block", (i[:, None] // HD == i[None, :] // HD))
    perm = np.zeros((P, P))
    for m in range(P):
        if m % 32 < 16:
            perm[m + 16, m] = -1
        else:
            perm[m - 16, m] = 1
    put("perm", perm)
    put("ntri", np.where(i[:, None] >= i[None, :], -1.0, 0.0))
    put("nones", -np.ones((P, P)))
    diag = (i[None, :] > i[:, None])
    causal = np.concatenate([diag, np.ones((P, P), bool), diag], axis=1)
    put("causal", causal)
    put("causal_neg", np.where(causal, 0.0, NEG))
    kk = np.arange(SEQ)
    put("window", np.concatenate([np.where(np.abs(kk[None, :] - (i[:, None] + q * P)) <= 128, 0.0, NEG) for q in range(2)], axis=1))
    t = np.arange(SEQ)
    inv = (np.float32(10000.0) ** (-np.arange(16, dtype=np.float32) / np.float32(16))).astype(np.float32)
    row, col = (t // GRID_W).astype(np.float32), (t % GRID_W).astype(np.float32)
    d = i % HD
    pos = np.where((d < 32)[:, None], row[None, :], col[None, :]).astype(np.float32)
    ang = (pos * inv[d % 16][:, None]).astype(np.float32)
    put("cos", np.cos(ang))
    put("sin", np.sin(ang))
    return out


def kernel(**inputs):
    import concourse.bacc as bacc
    from concourse.bass_utils import run_bass_kernel_spmd as run

    a = {k: np.asarray(v) for k, v in inputs.items()}
    f = np.float32

    kv_at = D + 4 * HD
    qkv = a["na_wqkv"][0]
    sw = a["swa_wqkv"][0]
    sw_q = sw[:, :D].reshape(D, HEADS, HD)[:, SWA_ORDER].reshape(D, D)
    sw_o = a["swa_wo"][0].reshape(HEADS, HD, D)[SWA_ORDER].reshape(D, D)
    parts = [pack_units(qkv[:, :2 * D], 8), pack_value_units(qkv[:, 2 * D:]), pack_units(a["na_wo"][0], 8)]

    def mlp(layer):
        w1, w2 = a["mlp_w1"][layer], a["mlp_w2"][layer]
        for k in range(2):
            cut = slice(k * DFF // 2, (k + 1) * DFF // 2)
            parts.append(pack_units(w1[:, cut], 8))
            parts.append(pack_units(w2[cut], 8))

    def ffn(layer):
        up = a["ffn_w_up_2"][layer]
        parts.append(pack_units(interleave(up[:, :DFF2], up[:, DFF2:]), 8))
        parts.append(pack_units(a["ffn_w_down_2"][layer], 8))

    mlp(0)
    parts += [pack_units(sw_q, 8), pack_units(sw[:, D:kv_at], 8), pack_value_units(sw[:, kv_at:]), pack_units(sw_o, 8)]
    mlp(1)
    parts += [pack_units(a["a_w_in_2"][0], 8), pack_units(interleave(a["a_w_glu_2"][0][:, :D], a["a_w_glu_2"][0][:, D:]), 8)]
    ffn(0)
    parts += [pack_units(a["w_kv_2"][:, :D], 8), pack_value_units(a["w_kv_2"][:, D:]), pack_units(a["b_w_q_2"][0], 8), pack_units(a["b_w_o_2"][0], 8)]
    ffn(1)
    weights = np.concatenate(parts)
    ada_w = np.concatenate([pack_units(a["ada_w"][k], 8) for k in range(2)])
    ada_b = np.repeat(columns(a["ada_b"]).reshape(P, 2, N_ADA, 1), 2, axis=3)

    x_t = np.concatenate([a["x"][0], a["ctx"][0]]).T.reshape(KT, P, TOK).transpose(1, 0, 2)
    two = lambda g, n: np.repeat(np.tile(g.reshape(HD), 2)[:, None], n, axis=1)
    dup = lambda g: np.repeat(columns(g), 2, axis=1)
    sinks = np.repeat(a["swa_sink"][0][SWA_ORDER][None, :], P, axis=0)
    cond = np.stack([columns(a["c"]), columns(a["c_ctx"])], axis=2).reshape(P, 16)
    vecs = np.concatenate([
        two(a["na_q_gain"], 8), two(a["na_k_gain"], 8), two(a["swa_q_gain"], 8), two(a["swa_k_gain"], 2),
        two(a["k_norm_2"], 8), two(a["b_q_norm_2"], 8), dup(a["g_mix"]), dup(a["g_mlp"]), columns(a["a_norm_2"]),
        columns(a["kv_norm_2"]), columns(a["b_norm_2"]), columns(a["ffn_norm_2"]), columns(a["a_d_2"]),
        columns(a["ffn_conv_w_2"]), columns(a["ffn_conv_b_2"]), sinks, cond], axis=1)
    assert vecs.shape[1] == N_VEC, (vecs.shape, N_VEC)

    q = np.arange(SEQ)
    r, c = q // GRID_W, q % GRID_W
    start = np.clip(c - 8, 0, GRID_W - 16)
    inside = (c[None, :] >= start[:, None]) & (c[None, :] < start[:, None] + 16)
    ri = r[None, :] - r[:, None] + 7
    ci = np.clip(c[None, :] - c[:, None] + 15, 0, 30)
    bias = np.where(inside[None], a["na_rpb"][0][:, ri, ci], f(NEG)).astype(f)
    bias = bias.reshape(HEADS, 2, P, SEQ).transpose(1, 0, 2, 3).reshape(2 * HEADS, P, SEQ)

    pair = lambda g: g.reshape(PAIRS, 2, STATES, -1).transpose(1, 2, 0, 3).reshape(P, PAIRS, -1)
    log_dt = np.repeat(a["a_log_dt_2"][0][:, None], STATES, axis=1)
    ssm_in = np.stack([pair(g)[:, :, 0] for g in (a["a_lam_re_2"][0], a["a_lam_im_2"][0], log_dt)], axis=1)
    ssm_bc = np.stack([pair(a["a_b_re_2"][0]), pair(a["a_b_im_2"][0]), pair(a["a_c_re_2"][0].transpose(0, 2, 1)),
                       pair(a["a_c_im_2"][0].transpose(0, 2, 1))], axis=1)

    nc = bacc.Bacc("TRN2", target_bir_lowering=False, num_devices=1)
    arrays = {"weights": weights, "ada_w": ada_w, "ada_b": ada_b, "x_t": x_t, "vecs": vecs, "cons": shape_constants(),
              "bias_na": bias, "ssm_in": ssm_in, "ssm_bc": ssm_bc}
    arrays = {k: np.ascontiguousarray(v) for k, v in arrays.items()}
    args = [nc.dram_tensor(k, v.shape, mybir.dt.from_np(v.dtype), kind="ExternalInput").ap() for k, v in arrays.items()]
    shapes = {"u_dram": (D, CH, NCH), "y_dram": (D, CH, NCH), "bat_dram": (NQ, P, QJ, 2, P), "ca_dram": (NQ, P, QJ, 2, P),
              "toep_dram": (NQ, P, 2 * QJ, P), "rot_dram": (P, 3, PAIRS, NCH)}
    scratch = [nc.dram_tensor(k, v, F32, kind="Internal").ap() for k, v in shapes.items()]
    out = nc.dram_tensor("out", (P, KT, SEQ), F32, kind="ExternalOutput").ap()
    program(nc, *args, scratch, out)
    got = run(nc, [arrays], core_ids=[0]).results[0]["out"]
    return np.ascontiguousarray(got.transpose(2, 1, 0).reshape(1, SEQ, D))
```
